# Optimizing a Trainium2 kernel written in Bass

```python
import jax, jax.numpy as jnp
from jax import lax
import numpy as np

D_MODEL = 1024
BATCH = 1
SEQ = 256
DEPTH = 2
DEC_BATCH = 8
DEC_SEQ = 1
PAST_LEN = 256
PAGE_SIZE = 128

N_HEADS = 8
HEAD_DIM = D_MODEL // N_HEADS
QKV_W = N_HEADS * HEAD_DIM
IDX_HEADS = 4
IDX_DIM = 64
TOPK_MAX = 256
IDX_Q_BLOCK = 64
ROPE_THETA = 10000.0
IDX_SCALE = (IDX_DIM * IDX_HEADS) ** -0.5
ATTN_IN_W = 3 * QKV_W + IDX_HEADS * IDX_DIM + IDX_DIM + IDX_HEADS
ATTN_SPLITS = (QKV_W, 2 * QKV_W, 3 * QKV_W, 3 * QKV_W + IDX_HEADS * IDX_DIM,
               3 * QKV_W + IDX_HEADS * IDX_DIM + IDX_DIM)
LRU_WIDTH = D_MODEL
LRU_BLOCKS = 8
LRU_BLOCK_W = LRU_WIDTH // LRU_BLOCKS
RG_C = 8.0
REC_CONV_W = 4
D_FF = 2816
FFN_CONV_W = 3
RMS_EPS = 1e-6
N_ATTN_LAYERS = (DEPTH + 1) // 2
N_REC_LAYERS = DEPTH // 2

kernel_name = "dsa_rglru_convffn_hybrid_step"

def rmsnorm(x, g):
    xf = x.astype(jnp.float32)
    y = xf * lax.rsqrt(jnp.mean(xf * xf, axis=-1, keepdims=True) + RMS_EPS) * g.astype(jnp.float32)
    return y.astype(x.dtype)

def rope(x, pos):
    d = x.shape[-1]
    half = d // 2
    inv = ROPE_THETA ** (-jnp.arange(half, dtype=jnp.float32) * 2.0 / d)
    ang = pos.astype(jnp.float32)[:, None] * inv[None, :]
    cos = jnp.cos(ang)[None, :, None, :]
    sin = jnp.sin(ang)[None, :, None, :]
    xf = x.astype(jnp.float32)
    x1, x2 = xf[..., :half], xf[..., half:]
    return jnp.concatenate([x1 * cos - x2 * sin, x2 * cos + x1 * sin], axis=-1).astype(x.dtype)

def causal_dwconv(x, buf, w, b):
    width = w.shape[0]
    t = x.shape[1]
    xp = jnp.concatenate([buf.astype(x.dtype), x], axis=1)
    y = b + sum(xp[:, k:k + t] * w[k] for k in range(width))
    return y, xp[:, -(width - 1):]

def attn_project(a, pos, w_in):
    bsz, t, _ = a.shape
    q, k, v, qi, ki, wi = jnp.split(a @ w_in, ATTN_SPLITS, axis=-1)
    q = rope(q.reshape(bsz, t, N_HEADS, HEAD_DIM), pos)
    k = rope(k.reshape(bsz, t, N_HEADS, HEAD_DIM), pos)
    v = v.reshape(bsz, t, N_HEADS, HEAD_DIM)
    qi = rope(qi.reshape(bsz, t, IDX_HEADS, IDX_DIM), pos)
    ki = rope(ki[:, :, None, :], pos)[:, :, 0]
    return q, k, v, qi, ki, wi

def indexer_topk(qi, wi, ki, q_pos, n_keys, topk):
    s = jnp.einsum('bqhd,bsd->bqhs', qi, ki, preferred_element_type=jnp.float32)
    score = jnp.einsum('bqhs,bqh->bqs', jax.nn.relu(s), wi.astype(jnp.float32)) * IDX_SCALE
    causal = jnp.arange(n_keys)[None, :] <= q_pos[:, None]
    score = jnp.where(causal[None], score, -jnp.inf)
    _, idx = lax.top_k(score, topk)
    valid = idx <= q_pos[None, :, None]
    return idx, valid

def sparse_attend(q, k_sel, v_sel, valid):
    logits = jnp.einsum('bqhd,bqkhd->bqhk', q, k_sel, preferred_element_type=jnp.float32) * (HEAD_DIM ** -0.5)
    logits = jnp.where(valid[:, :, None, :], logits, -jnp.inf)
    p = jax.nn.softmax(logits, axis=-1)
    return jnp.einsum('bqhk,bqkhd->bqhd', p.astype(v_sel.dtype), v_sel)

def dsa_prompt(q, k, v, qi, ki, wi):
    bsz, s = q.shape[:2]
    topk = min(TOPK_MAX, s // 4)
    nb = s // IDX_Q_BLOCK
    gather = jax.vmap(lambda src, ib: src[ib])

    def blk(args):
        qb, qib, wib, start = args
        q_pos = start + jnp.arange(IDX_Q_BLOCK)
        idx, valid = indexer_topk(qib, wib, ki, q_pos, s, topk)
        return sparse_attend(qb, gather(k, idx), gather(v, idx), valid)

    to_blocks = lambda t: jnp.moveaxis(t.reshape(bsz, nb, IDX_Q_BLOCK, *t.shape[2:]), 1, 0)
    out = lax.map(blk, (to_blocks(q), to_blocks(qi), to_blocks(wi), jnp.arange(nb) * IDX_Q_BLOCK))
    return jnp.moveaxis(out, 0, 1).reshape(bsz, s, N_HEADS, HEAD_DIM)

def dsa_sample(q, k_new, v_new, qi, ki_new, wi, pool_k, pool_v, pool_ki, layer, page_table):
    db, t = q.shape[:2]
    past = page_table.shape[1] * PAGE_SIZE
    n_keys = past + t
    topk = min(TOPK_MAX, n_keys // 4)
    ki_past = pool_ki[layer, page_table].reshape(db, past, IDX_DIM)
    ki_all = jnp.concatenate([ki_past.astype(ki_new.dtype), ki_new], axis=1)
    q_pos = past + jnp.arange(t)
    idx, valid = indexer_topk(qi, wi, ki_all, q_pos, n_keys, topk)
    in_past = idx < past
    pidx = jnp.minimum(idx, past - 1)
    phys = jnp.take_along_axis(page_table, (pidx // PAGE_SIZE).reshape(db, -1), axis=1).reshape(idx.shape)
    off = pidx % PAGE_SIZE
    nidx = jnp.clip(idx - past, 0, t - 1)
    gather = jax.vmap(lambda src, ib: src[ib])

    def pick(pool, new):
        old = pool[layer, phys, off].astype(new.dtype)
        return jnp.where(in_past[..., None, None], old, gather(new, nidx))

    return sparse_attend(q, pick(pool_k, k_new), pick(pool_v, v_new), valid)

def block_diag(x, w):
    xb = x.reshape(*x.shape[:-1], LRU_BLOCKS, LRU_BLOCK_W)
    return jnp.einsum('btnc,ncd->btnd', xb, w).reshape(x.shape)

def rglru_mixer(a, conv_buf, h0, w_in, w_conv, b_conv, w_ga, b_ga, w_gx, b_gx, lam, w_out):
    gate, xb = jnp.split(a @ w_in, 2, axis=-1)
    xc, new_buf = causal_dwconv(xb, conv_buf, w_conv, b_conv)
    r = jax.nn.sigmoid((block_diag(xc, w_ga) + b_ga).astype(jnp.float32))
    ig = jax.nn.sigmoid((block_diag(xc, w_gx) + b_gx).astype(jnp.float32))
    log_a = -RG_C * r * jax.nn.softplus(-lam.astype(jnp.float32))
    a_t = jnp.exp(log_a)
    b_t = jnp.sqrt(-jnp.expm1(2.0 * log_a)) * ig * xc.astype(jnp.float32)

    def step(h, ab):
        h = ab[0] * h + ab[1]
        return h, h

    h_last, hs = lax.scan(step, h0.astype(jnp.float32), (jnp.swapaxes(a_t, 0, 1), jnp.swapaxes(b_t, 0, 1)))
    hs = jnp.swapaxes(hs, 0, 1).astype(a.dtype)
    y = (jax.nn.gelu(gate) * hs) @ w_out
    return y, new_buf, h_last.astype(a.dtype)

def conv_ffn(a, buf, w_up, w_conv, b_conv, w_down):
    gate, val = jnp.split(a @ w_up, 2, axis=-1)
    gate_c, new_buf = causal_dwconv(gate, buf, w_conv, b_conv)
    return (jax.nn.gelu(gate_c) * val) @ w_down, new_buf

def setup_inputs(seed: int = 0) -> dict:
    key = jax.random.key(seed)
    ks = jax.random.split(key, 32)
    n_pages = PAST_LEN // PAGE_SIZE
    n_used = DEC_BATCH * n_pages
    n_phys = n_used + max(1, n_used // 4)
    f32 = jnp.float32
    nrm = lambda k, shape, scale: jax.random.normal(k, shape, f32) * scale
    lru_base = jax.random.uniform(ks[21], (N_REC_LAYERS, LRU_WIDTH), f32, 0.9, 0.999)
    return {
        "x_prompt": nrm(ks[0], (BATCH, SEQ, D_MODEL), 1.0),
        "x_sample": nrm(ks[1], (DEC_BATCH, DEC_SEQ, D_MODEL), 1.0),
        "cache_k": nrm(ks[2], (N_ATTN_LAYERS, n_phys, PAGE_SIZE, N_HEADS, HEAD_DIM), 1.0),
        "cache_v": nrm(ks[3], (N_ATTN_LAYERS, n_phys, PAGE_SIZE, N_HEADS, HEAD_DIM), 1.0),
        "cache_kidx": nrm(ks[4], (N_ATTN_LAYERS, n_phys, PAGE_SIZE, IDX_DIM), 1.0),
        "state_lru_h": nrm(ks[5], (N_REC_LAYERS, DEC_BATCH, LRU_WIDTH), 0.5),
        "state_lru_conv": nrm(ks[6], (N_REC_LAYERS, DEC_BATCH, REC_CONV_W - 1, LRU_WIDTH), 1.0),
        "state_ffn_conv": nrm(ks[7], (DEPTH, DEC_BATCH, FFN_CONV_W - 1, D_FF), 1.0),
        "page_table": jax.random.permutation(ks[8], n_phys)[:n_used].reshape(DEC_BATCH, n_pages).astype(jnp.int32),
        "norm_mix": 1.0 + nrm(ks[9], (DEPTH, D_MODEL), 0.02),
        "norm_ffn": 1.0 + nrm(ks[10], (DEPTH, D_MODEL), 0.02),
        "norm_final": 1.0 + nrm(ks[11], (D_MODEL,), 0.02),
        "w_attn_in": nrm(ks[12], (N_ATTN_LAYERS, D_MODEL, ATTN_IN_W), D_MODEL ** -0.5),
        "w_attn_out": nrm(ks[13], (N_ATTN_LAYERS, QKV_W, D_MODEL), QKV_W ** -0.5),
        "w_rec_in": nrm(ks[14], (N_REC_LAYERS, D_MODEL, 2 * LRU_WIDTH), D_MODEL ** -0.5),
        "w_rec_conv": nrm(ks[15], (N_REC_LAYERS, REC_CONV_W, LRU_WIDTH), REC_CONV_W ** -0.5),
        "b_rec_conv": nrm(ks[16], (N_REC_LAYERS, LRU_WIDTH), 0.01),
        "w_gate_a": nrm(ks[17], (N_REC_LAYERS, LRU_BLOCKS, LRU_BLOCK_W, LRU_BLOCK_W), LRU_BLOCK_W ** -0.5),
        "b_gate_a": nrm(ks[18], (N_REC_LAYERS, LRU_WIDTH), 0.01),
        "w_gate_x": nrm(ks[19], (N_REC_LAYERS, LRU_BLOCKS, LRU_BLOCK_W, LRU_BLOCK_W), LRU_BLOCK_W ** -0.5),
        "b_gate_x": nrm(ks[20], (N_REC_LAYERS, LRU_WIDTH), 0.01),
        "lru_lambda": jnp.log(lru_base) - jnp.log1p(-lru_base),
        "w_rec_out": nrm(ks[22], (N_REC_LAYERS, LRU_WIDTH, D_MODEL), LRU_WIDTH ** -0.5),
        "w_ffn_up": nrm(ks[23], (DEPTH, D_MODEL, 2 * D_FF), D_MODEL ** -0.5),
        "w_ffn_conv": nrm(ks[24], (DEPTH, FFN_CONV_W, D_FF), FFN_CONV_W ** -0.5),
        "b_ffn_conv": nrm(ks[25], (DEPTH, D_FF), 0.01),
        "w_ffn_down": nrm(ks[26], (DEPTH, D_FF, D_MODEL), D_FF ** -0.5),
    }

def reference(x_prompt, x_sample, cache_k, cache_v, cache_kidx, state_lru_h, state_lru_conv, state_ffn_conv,
              page_table, norm_mix, norm_ffn, norm_final, w_attn_in, w_attn_out, w_rec_in, w_rec_conv,
              b_rec_conv, w_gate_a, b_gate_a, w_gate_x, b_gate_x, lru_lambda, w_rec_out, w_ffn_up,
              w_ffn_conv, b_ffn_conv, w_ffn_down):
    bsz, s, _ = x_prompt.shape
    db, t, _ = x_sample.shape
    past = page_table.shape[1] * PAGE_SIZE
    pos_p = jnp.arange(s)
    pos_s = past + jnp.arange(t)
    hp, hs = x_prompt, x_sample
    kp, vp, kip, ksm, vsm, kism = [], [], [], [], [], []
    lhp, lcp, lhs, lcs = [], [], [], []
    fcp, fcs = [], []
    for i in range(DEPTH):
        j = i // 2
        ap = rmsnorm(hp, norm_mix[i])
        asm = rmsnorm(hs, norm_mix[i])
        if i % 2 == 0:
            q, k, v, qi, ki, wi = attn_project(ap, pos_p, w_attn_in[j])
            o = dsa_prompt(q, k, v, qi, ki, wi)
            hp = hp + o.reshape(bsz, s, QKV_W) @ w_attn_out[j]
            kp.append(k); vp.append(v); kip.append(ki)
            q, k, v, qi, ki, wi = attn_project(asm, pos_s, w_attn_in[j])
            o = dsa_sample(q, k, v, qi, ki, wi, cache_k, cache_v, cache_kidx, j, page_table)
            hs = hs + o.reshape(db, t, QKV_W) @ w_attn_out[j]
            ksm.append(k); vsm.append(v); kism.append(ki)
        else:
            rec = (w_rec_in[j], w_rec_conv[j], b_rec_conv[j], w_gate_a[j], b_gate_a[j],
                   w_gate_x[j], b_gate_x[j], lru_lambda[j], w_rec_out[j])
            o, cb, hl = rglru_mixer(ap, jnp.zeros((bsz, REC_CONV_W - 1, LRU_WIDTH), ap.dtype),
                                    jnp.zeros((bsz, LRU_WIDTH), ap.dtype), *rec)
            hp = hp + o
            lhp.append(hl); lcp.append(cb)
            o, cb, hl = rglru_mixer(asm, state_lru_conv[j], state_lru_h[j], *rec)
            hs = hs + o
            lhs.append(hl); lcs.append(cb)
        ffn = (w_ffn_up[i], w_ffn_conv[i], b_ffn_conv[i], w_ffn_down[i])
        o, fb = conv_ffn(rmsnorm(hp, norm_ffn[i]), jnp.zeros((bsz, FFN_CONV_W - 1, D_FF), hp.dtype), *ffn)
        hp = hp + o
        fcp.append(fb)
        o, fb = conv_ffn(rmsnorm(hs, norm_ffn[i]), state_ffn_conv[i], *ffn)
        hs = hs + o
        fcs.append(fb)
    y_prompt = rmsnorm(hp, norm_final)
    y_sample = rmsnorm(hs, norm_final)
    new_k_prompt = jnp.stack(kp)
    new_v_prompt = jnp.stack(vp)
    new_kidx_prompt = jnp.stack(kip)
    new_k_sample = jnp.stack(ksm)
    new_v_sample = jnp.stack(vsm)
    new_kidx_sample = jnp.stack(kism)
    lru_h_prompt = jnp.stack(lhp)
    lru_conv_prompt = jnp.stack(lcp)
    lru_h_sample = jnp.stack(lhs)
    lru_conv_sample = jnp.stack(lcs)
    ffn_conv_prompt = jnp.stack(fcp)
    ffn_conv_sample = jnp.stack(fcs)
    return (y_prompt, y_sample, new_k_prompt, new_v_prompt, new_kidx_prompt, new_k_sample, new_v_sample,
            new_kidx_sample, lru_h_prompt, lru_conv_prompt, lru_h_sample, lru_conv_sample,
            ffn_conv_prompt, ffn_conv_sample)


_drawn_inputs = setup_inputs


def setup_inputs(seed=0):
    import zlib

    import numpy as np

    out = dict(_drawn_inputs(seed))
    spreads = {}
    factors = {'norm_final': 7.991, 'b_gate_a': 25.861, 'b_gate_x': 8.0, 'b_ffn_conv': 7.291}
    for name, (base, spread) in spreads.items():
        noise = np.random.default_rng([zlib.crc32(name.encode()), seed]).standard_normal(out[name].shape)
        drawn = base * np.exp(spread * noise) if base else spread * noise
        out[name] = __import__('jax').numpy.asarray(drawn.astype(out[name].dtype))
    for name, factor in factors.items():
        out[name] = (out[name] * factor).astype(out[name].dtype)
    return out
```

```python
from contextlib import ExitStack

import concourse.bass as bass
from concourse import mybir

ALU = mybir.AluOpType
ACT = mybir.ActivationFunctionType
AX = mybir.AxisListType
F32 = mybir.dt.float32
F16 = mybir.dt.float16
I32 = mybir.dt.int32
U32 = mybir.dt.uint32

P = 128
D = 1024
DC = D // P
TP = 256
NS = 8
T = TP + NS
H = 8
PAST = 256
PAGE = 128
IH, ID = 4, 64
TOPK = 64
DFF = 2816
FC = DFF // P
WSCALE = 512.0
INV = 1.0 / WSCALE
SCALE = float(P) ** -0.5
IDX_SCALE = float(ID * IH) ** -0.5
EPS = 1e-6
RG_C = 8.0
OUT_OF_REACH = -1.0e30
TAKEN = -3.0e38
SLOTS = 4

R_IDX, R_Q, R_K, R_V, R_OUT = 0, 1, 3, 5, 7
R_UP = (9, 30)
R_DOWN = (20, 41)
R_XB, R_GATE, R_ROUT = 24, 26, 28
ROUNDS = 45
UP_ROUNDS = FC // 2
DOWN_HALF = FC // 2

ROW_NORM = 0
ROW_CONV_STATE = 5
ROW_H0 = 29
ROW_CONV_W = 37
ROW_CONV_B, ROW_GA_B, ROW_GX_B, ROW_LAMBDA = 41, 42, 43, 44
ROWS_REC = 45
FROW_STATE, FROW_W, FROW_B, ROWS_FFN = 0, 16, 19, 20

CA_IDENT, CA_COSH, CA_SINH, CA_COSI, CA_SINI, CA_IOTA = 0, P, P + T, P + 2 * T, P + 3 * T, P + 4 * T
CA_W = CA_IOTA + 1
CB_PAIR, CB_REP, CB_SAME, CB_HEAD, CB_W = 0, 512, 544, 552, 616


def unit_shapes(rnd):
    if rnd == R_IDX:
        return [(DC, P), (DC, P), (DC, ID), (DC, IH)]
    if any(r <= rnd < r + 4 for r in R_DOWN):
        return [(DOWN_HALF, P)] * 4
    return [(DC, P)] * 4


class Steps:

    def __init__(self, eng, sem):
        self.eng, self.sem, self.n = eng, sem, 0

    def done(self, ins):
        ins.then_inc(self.sem, 1)
        self.n = self.n + 1

    def wait(self):
        self.eng.wait_ge(self.sem, self.n)


def build(nc, a, o):
    with ExitStack() as ctx:
        def sb(name, shape, dt=F32):
            return ctx.enter_context(nc.sbuf_tensor(name, shape, dt))

        def sem(name):
            return ctx.enter_context(nc.semaphore(name))

        stage = sb("stage", [P, SLOTS, DOWN_HALF, P])
        w_hi = sb("w_hi", [P, SLOTS, DOWN_HALF, P], F16)
        w_lo = sb("w_lo", [P, SLOTS, DOWN_HALF, P], F16)
        hT = sb("hT", [P, DC, T])
        aH = sb("aH", [P, DC, T], F16)
        aL = sb("aL", [P, DC, T], F16)
        zH = sb("zH", [P, FC, T], F16)
        zL = sb("zL", [P, FC, T], F16)
        a32 = sb("a32", [P, 2, T])
        sq = sb("sq", [P, 2, T])
        sqsum = sb("sqsum", [P, T])
        root = sb("root", [P, T])
        rinv = sb("rinv", [P, T])
        work = sb("work", [P, 4 * T])
        c32 = work[:, 0:2 * T].rearrange("p (b t) -> p b t", b=2)
        z32 = work[:, 2 * T:].rearrange("p (b t) -> p b t", b=2)
        area1 = sb("area1", [P, 8192])
        area2 = sb("area2", [P, 2 * DC * T])
        area3 = sb("area3", [P, 2 * 2 * D])
        xtok = area1[:, 0:2048].rearrange("p (t d) -> p t d", t=2)
        xsmp = area1[0:NS, 2048:3072]
        kgat = area1[:, 0:4096].rearrange("p (j d) -> p j d", j=4)
        vgat = area1[:, 4096:8192].rearrange("p (j d) -> p j d", j=4)
        xc = area1[:, 0:DC * T].rearrange("p (c t) -> p c t", c=DC)
        ix = area1[:, DC * T:2 * DC * T].rearrange("p (c t) -> p c t", c=DC)
        gateT = area1[:, 2 * DC * T:3 * DC * T].rearrange("p (c t) -> p c t", c=DC)
        ytok = area1[:, 0:2048].rearrange("p (t d) -> p t d", t=2)
        ysmp = area1[0:NS, 2048:3072]
        qT = area2[:, 0:DC * T].rearrange("p (c t) -> p c t", c=DC)
        kT = area2[:, DC * T:].rearrange("p (c t) -> p c t", c=DC)
        decay, bq = qT, kT
        yT = qT
        ktok = area3[:, 0:2048].rearrange("p (t d) -> p t d", t=2)
        vtok = area3[:, 2048:4096].rearrange("p (t d) -> p t d", t=2)
        hsT = area3[:, 0:DC * T].rearrange("p (c t) -> p c t", c=DC)
        rows = area3[0:10, 0:DFF]
        frow = [area2[0:ROWS_FFN, 0:DFF], area1[0:ROWS_FFN, 3072:3072 + DFF]]
        rowsR = area3[0:ROWS_REC, 0:D].rearrange("r (c p) -> r c p", c=DC)
        rrows = sb("rrows", [11, D])
        hrows = sb("hrows", [9, D])
        ksmp, vsmp = rrows[0:NS, :], hrows[0:NS, :]
        scratch = sb("scratch", [P, 4096])
        gstage = scratch[:, 0:2048].rearrange("p (g c n) -> p g c n", g=2, c=DC)
        g_hi = scratch[:, 2048:3072].bitcast(F16).rearrange("p (g c n) -> p g c n", g=2, c=DC)
        g_lo = scratch[:, 3072:4096].bitcast(F16).rearrange("p (g c n) -> p g c n", g=2, c=DC)
        prm = sb("prm", [P, DC, ROWS_REC])
        fprm = [sb(f"fprm{i}", [P, FC, ROWS_FFN]) for i in range(2)]
        fw = [sb(f"fw{i}", [P, FC, 3]) for i in range(2)]
        fpre = [sb(f"fpre{i}", [P, FC, NS]) for i in range(2)]
        ftmp = sb("ftmp", [P, FC, NS])
        rw = sb("rw", [P, DC, 4])
        rpre = sb("rpre", [P, DC, NS])
        rtmp = sb("rtmp", [P, DC, NS])
        spl = sb("spl", [P, 12, DC])
        tails = sb("tails", [P, FC, 11])
        ca = sb("ca", [P, CA_W])
        cb = sb("cb", [32, CB_W])
        ones = sb("ones", [P, P])
        epsc = sb("epsc", [P, 1])
        prod = scratch[:, 0:1024]
        qsmp = scratch[0:NS, 1024:2048]
        pT = scratch[:, 2048:2816].rearrange("p (b n) -> p b n", b=2)
        vT = scratch[:, 2816:2816 + 2 * T].rearrange("p (b t) -> p b t", b=2)
        rot = scratch[:, 3344:3344 + 2 * T].rearrange("p (b t) -> p b t", b=2)
        lg = work[:, 0:768].rearrange("p (b n) -> p b n", b=2)
        relu1 = area1[:, 5888:6912].rearrange("p (h k) -> p h k", h=IH)
        relu0 = area1[:, 6912:7424].rearrange("p (h k) -> p h k", h=IH)
        kx = area3[:, 1024:2048].rearrange("p (g n) -> p g n", g=2)
        kxT = area3[:, 2048:2048 + 4 * (PAST + 1)].rearrange("p (j n) -> p j n", j=4)
        spareH = zH[:, DC:FC, :].rearrange("p c t -> p (c t)").bitcast(F32)
        spareL = zL[:, DC:FC, :].rearrange("p c t -> p (c t)").bitcast(F32)
        qiT = spareH[:, 0:2 * T].rearrange("p (b t) -> p b t", b=2)
        kiT = spareH[:, 2 * T:3 * T]
        wiT = spareH[0:IH, 3 * T:4 * T]
        score = spareH[:, 4 * T:4 * T + 384]
        abias = spareH[:, 4 * T + 384:4 * T + 768]
        sR = spareL[0:32, 0:PAST + 1]
        sscore = spareL[0:NS, 258:258 + PAST + 1]
        sl = spareL[0:NS, 516:1028]
        phys2 = spareL[0:NS, 1028:1156]
        flag2 = spareL[0:NS, 1156:1284]
        vnew = sb("vnew", [P, H, NS])
        kitok = sb("kitok", [P, 2, ID])
        kismp = sb("kismp", [NS, ID])
        wtok = sb("wtok", [P, 2, IH])
        top8 = sb("top8", [P, 8])
        nmx = sb("nmx", [P, 2, 2])
        psum_e = sb("psum_e", [P, 2, 2])
        prcp = sb("prcp", [P, 2, 2])
        ptb = sb("ptb", [P, 2 * NS], I32)
        pt8 = sb("pt8", [NS, 2], I32)
        pt8f = sb("pt8f", [NS, 4])
        gidx = sb("gidx", [P, 2 * NS], U32)
        qz = sb("qz", [P, 4, 32])
        wblk = sb("wblk", [32, NS])
        s8 = sb("s8", [NS, 8])
        i8 = sb("i8", [NS, TOPK], U32)
        idxf = sb("idxf", [NS, TOPK])
        idxt = sb("idxt", [NS, TOPK])
        selnew = sb("selnew", [NS, 2])
        seld = sb("seld", [NS, NS])
        gix = sb("gix", [P, 4], U32)
        gbias = sb("gbias", [P, 4])
        qk = sb("qk", [P, 4, H])
        qkb = sb("qkb", [P, 4, H])
        nprod = sb("nprod", [P, H * NS])
        nl = sb("nl", [NS, 64])
        lnew = sb("lnew", [NS, NS])
        lnew2 = sb("lnew2", [NS, NS])
        smx = sb("smx", [NS, NS])
        ssum = sb("ssum", [NS, NS])
        pnew = sb("pnew", [NS, NS])
        pnd = sb("pnd", [NS, 64])
        pb = sb("pb", [P, 4, H, 2])
        onew = sb("onew", [P, H * NS])
        onw2 = sb("onw2", [P, H * NS])
        gates = area1[:, 3 * DC * T:3 * DC * T + 4 * T].rearrange("p (b g t) -> p b g t", b=2, g=2)
        y32 = c32

        acc = ctx.enter_context(nc.psum_tensor("acc", [P, SLOTS, 512], F32))
        misc = ctx.enter_context(nc.psum_tensor("misc", [P, 4, 512], F32))
        A, B, C, E = (misc[:, i, :] for i in range(4))
        AB = misc[:, 0:2, :]
        ident = ca[:, CA_IDENT:CA_IDENT + P]

        loaded = [sem(f"loaded{s}") for s in range(SLOTS)]
        hi_done, lo_done = sem("hi_done"), sem("lo_done")
        unit_done = sem("unit_done")
        acc_read = sem("acc_read")
        x_in, const_in, prm_in, f_in, pt_in = sem("x_in"), sem("const_in"), sem("prm_in"), sem("f_in"), sem("pt_in")
        f1_in, g_in, xs_in, x0_in = sem("f1_in"), sem("g_in"), sem("xs_in"), sem("x0_in")
        x_turned, x_kept = sem("x_turned"), sem("x_kept")
        prm_turned, prm_kept, prm_ready = sem("prm_turned"), sem("prm_kept"), sem("prm_ready")
        fprm_turned, fprm_kept = sem("fprm_turned"), sem("fprm_kept")
        sq_done, ss_done = sem("sq_done"), sem("ss_done")
        rms_sum, rms_root, a_full, a_hi, a_lo = (sem(n) for n in ("rms_sum", "rms_root", "a_full", "a_hi", "a_lo"))
        dve_step, pool_step, act_step = sem("dve_step"), sem("pool_step"), sem("act_step")
        ones_set = sem("ones_set")
        conv0, gelu_done, z_hi, z_lo = sem("conv0"), sem("gelu_done"), sem("z_hi"), sem("z_lo")
        tail_turned, tail_kept = sem("tail_turned"), sem("tail_kept")
        stored, kv_stored, f_stored = sem("stored"), sem("kv_stored"), sem("f_stored")
        sscore_kept = sem("sscore_kept")
        roped = sem("roped")
        ki_twice, wi_turned, ki_kept, wtok_done = sem("ki_twice"), sem("wi_turned"), sem("ki_kept"), sem("wtok_done")
        idx_mm, idx_relu, idx_sum, idx_masked = sem("idx_mm"), sem("idx_relu"), sem("idx_sum"), sem("idx_masked")
        bias_done, bias_masked = sem("bias_done"), sem("bias_masked")
        gidx_done, kx_turned, kx_kept = sem("gidx_done"), sem("kx_turned"), sem("kx_kept")
        kx_in = [sem(f"kx_in{i}") for i in range(2)]
        kg_in = [sem(f"kg_in{i}") for i in range(4)]
        vg_in = [sem(f"vg_in{i}") for i in range(4)]
        qz_zero, qz_done, wrep_mm, wblk_done = sem("qz_zero"), sem("qz_done"), sem("wrep_mm"), sem("wblk_done")
        ss_mm, ss_relu, sc_mm = sem("ss_mm"), sem("ss_relu"), sem("sc_mm")
        phys_done, phys_turned, gix_done = sem("phys_done"), sem("phys_turned"), sem("gix_done")
        qs_turned, qs_kept, qb_mm, qb_read = sem("qs_turned"), sem("qs_kept"), sem("qb_mm"), sem("qb_read")
        kv_turned, kv_kept, v_full = sem("kv_turned"), sem("kv_kept"), sem("v_full")
        sl_turned, nprod_done, sl_kept, smx_done, sexp_done = (
            sem(n) for n in ("sl_turned", "nprod_done", "sl_kept", "smx_done", "sexp_done"))
        sp_done, sp_turned, pb_done, so_mm, so_done, so_hi = (
            sem(n) for n in ("sp_done", "sp_turned", "pb_done", "so_mm", "so_done", "so_hi"))
        lg_mm, lg_max, p_exp, p_rcp, p_norm, p_turned, p_kept, o_mm, o_hi, o_lo = (
            sem(n) for n in ("lg_mm", "lg_max", "p_exp", "p_rcp", "p_norm", "p_turned", "p_kept", "o_mm", "o_hi", "o_lo"))
        rc0, xc_full, xc_hi, xc_lo, g_hi_done, g_lo_done = (
            sem(n) for n in ("rc0", "xc_full", "xc_hi", "xc_lo", "g_hi_done", "g_lo_done"))
        gate_mm, gate_halved, gate_sig, gate_tanh, bq_done, ix_done, b_root, b_full, hs_done = (
            sem(n) for n in ("gate_mm", "gate_halved", "gate_sig", "gate_tanh", "bq_done", "ix_done", "b_root", "b_full", "hs_done"))
        ggelu, y_full, y_hi, y_lo = sem("ggelu"), sem("y_full"), sem("y_hi"), sem("y_lo")
        rt_turned, rt_kept = sem("rt_turned"), sem("rt_kept")
        yt_full, yt_turned, yt_kept = sem("yt_full"), sem("yt_turned"), sem("yt_kept")
        sp_exp = sem("sp_exp")

        def blocks(w):
            return w.rearrange("(c p) n -> p c n", p=P)

        w_in = blocks(a["w_attn_in"][0])
        w_out = blocks(a["w_attn_out"][0])
        w_rin = blocks(a["w_rec_in"][0])
        w_rout = blocks(a["w_rec_out"][0])
        w_up = [blocks(a["w_ffn_up"][i]) for i in range(2)]
        w_down = [blocks(a["w_ffn_down"][i]) for i in range(2)]
        Q0 = 3 * D
        stores = [0]

        block = ctx.enter_context(nc.Block())

        @block.sync
        def _(sp):
            def load(u, s, m, w, col, cols, first=0, n=DC):
                if not (isinstance(u, int) and u < SLOTS):
                    sp.wait_ge(lo_done, u - SLOTS + 1)
                sp.dma_start(stage[:, s, 0:n, 0:cols], w[:, first:first + n, col]).then_inc(loaded[s], 16)

            def store(dst, src, done=stored):
                sp.dma_start(dst, src).then_inc(done, 16)
                stores[0] += done is stored

            sp.dma_start(xtok[:, 0, :], a["x_prompt"][0, 0:P, :]).then_inc(x0_in, 16)
            sp.dma_start(ca[:], a["const_a"]).then_inc(const_in, 16)
            sp.dma_start(xtok[:, 1, :], a["x_prompt"][0, P:TP, :]).then_inc(x_in, 16)
            load(0, 0, 0, w_in, bass.ds(Q0, P), P)
            load(1, 1, 0, w_in, bass.ds(Q0 + P, P), P)
            load(2, 2, 0, w_in, bass.ds(Q0 + IH * ID, ID), ID)
            load(3, 3, 0, w_in, bass.ds(Q0 + IH * ID + ID, IH), IH)
            with sp.Fori(0, R_OUT - R_Q) as i:
                for s in range(SLOTS):
                    load(i * 4 + (4 * R_Q + s), s, i + R_Q, w_in, bass.ds(i * 512 + s * P, P), P)
            sp.wait_ge(ki_kept, 2)
            store(o["new_kidx_prompt"][0, 0].rearrange("(t p) d -> p t d", p=P), kitok[:])
            store(o["new_kidx_sample"][0].rearrange("s a d -> (s a) d"), kismp[:])
            for s in range(SLOTS):
                load(4 * R_OUT + s, s, R_OUT, w_out, bass.ds(s * P, P), P)
            for s in range(SLOTS):
                load(4 * R_OUT + 4 + s, s, R_OUT + 1, w_out, bass.ds((4 + s) * P, P), P)
            sp.wait_ge(kv_kept, 2 * 2 * H)
            for t in range(2):
                store(o["new_k_prompt"][0, 0, t * P:(t + 1) * P].rearrange("p h d -> p (h d)"), ktok[:, t, :], kv_stored)
                store(o["new_v_prompt"][0, 0, t * P:(t + 1) * P].rearrange("p h d -> p (h d)"), vtok[:, t, :], kv_stored)
            store(o["new_k_sample"][0].rearrange("s a h d -> (s a) (h d)"), ksmp, kv_stored)
            store(o["new_v_sample"][0].rearrange("s a h d -> (s a) (h d)"), vsmp, kv_stored)

            def ffn(layer):
                r0 = R_UP[layer]
                with sp.Fori(0, UP_ROUNDS) as i:
                    for s in range(SLOTS):
                        load(i * 4 + (4 * r0 + s), s, i + r0, w_up[layer],
                             bass.ds(i * 256 + (s // 2 * P + s % 2 * DFF), P), P)
                r0 = R_DOWN[layer]
                with sp.Fori(0, 4) as i:
                    for s in range(SLOTS):
                        load(i * 4 + (4 * r0 + s), s, i + r0, w_down[layer],
                             bass.ds(i * 256 + s // 2 * P, P), P, first=s % 2 * DOWN_HALF, n=DOWN_HALF)

            def ffn_state(layer):
                sp.wait_ge(tail_kept, 2 * layer + 2)
                store(o["ffn_conv_prompt"][layer, 0], rows[0:2, :], f_stored)
                store(o["ffn_conv_sample"][layer, :, 1, :], rows[2:10, :], f_stored)

            ffn(0)
            for r in range(4):
                for s in range(SLOTS):
                    u = 4 * (R_XB + r) + s
                    load(u, s, R_XB + r, w_rin, bass.ds((D if r < 2 else 0) + (4 * (r % 2) + s) * P, P), P)
                if r == 0:
                    ffn_state(0)
            for r in range(2):
                for s in range(SLOTS):
                    load(4 * (R_ROUT + r) + s, s, R_ROUT + r, w_rout, bass.ds((4 * r + s) * P, P), P)
            ffn(1)
            sp.wait_ge(rt_kept, 2)
            store(o["lru_conv_prompt"][0, 0], rrows[0:3, :])
            store(o["lru_conv_sample"][0, :, 2, :], rrows[3:11, :])
            store(o["lru_h_prompt"][0], hrows[0:1, :])
            store(o["lru_h_sample"][0], hrows[1:9, :])
            ffn_state(1)
            sp.wait_ge(yt_kept, DC)
            store(o["y_prompt"][0].rearrange("(t p) d -> p t d", p=P), ytok)
            store(o["y_sample"].rearrange("s a d -> (s a) d"), ysmp)
            copies = 3
            sp.wait_ge(stored, 16 * (stores[0] + copies))
            sp.wait_ge(kv_stored, 16 * 6)
            sp.wait_ge(f_stored, 16 * 4)

        @block.scalar
        def _(act):
            steps = Steps(act, act_step)

            def hi(u, s, m, shape):
                n, cols = shape
                act.wait_ge(loaded[s], 16 * m + 16)
                if not (isinstance(u, int) and u < SLOTS):
                    act.wait_ge(unit_done, u - SLOTS + 1)
                nc.scalar.activation(w_hi[:, s, 0:n, 0:cols], stage[:, s, 0:n, 0:cols], ACT.Copy,
                                     scale=WSCALE).then_inc(hi_done, 1)

            def square(g, p, n, acc_count):
                act.wait_ge(acc_read, acc_count)
                if not (isinstance(g, int) and g < 2):
                    act.wait_ge(ss_done, g - 1)
                nc.scalar.activation(sq[:, p, :], hT[:, n, :] if isinstance(n, int) else hT[:, bass.ds(n, 1), :],
                                     ACT.Square).then_inc(sq_done, 1)

            def norm_root(k):
                act.wait_ge(rms_sum, k + 1)
                nc.scalar.activation(root[:], E[:, 0:T], ACT.Sqrt, bias=epsc[:, 0:1], scale=1.0 / D).then_inc(rms_root, 1)

            def norm_hi(k):
                for c in range(DC):
                    act.wait_ge(a_full, DC * k + c + 1)
                    nc.scalar.activation(aH[:, c, :], a32[:, c % 2, :], ACT.Copy).then_inc(a_hi, 1)

            act.dma_start(xsmp, a["x_sample"].rearrange("s a d -> (s a) d")).then_inc(xs_in, 16)
            act.dma_start(cb[:], a["const_b"]).then_inc(xs_in, 16)
            act.dma_start(pt8[:], a["page_table"]).then_inc(pt_in, 16)
            act.dma_start(ptb[:], a["page_table"].rearrange("(a s) g -> a (s g)", a=1).partition_broadcast(P)
                          ).then_inc(pt_in, 16)
            prow = area3[:, 0:D]

            def row(r, n, src):
                act.dma_start(prow[r:r + n, :], src).then_inc(prm_in, 16)

            row(0, 1, a["norm_mix"][0:1, :])
            row(1, 1, a["norm_ffn"][0:1, :])
            row(2, 1, a["norm_mix"][1:2, :])
            row(3, 1, a["norm_ffn"][1:2, :])
            row(4, 1, a["norm_final"].rearrange("(a d) -> a d", a=1))
            row(ROW_CONV_STATE, 24, a["state_lru_conv"][0].rearrange("s k d -> (s k) d"))
            row(ROW_H0, NS, a["state_lru_h"][0])
            row(ROW_CONV_W, 4, a["w_rec_conv"][0])
            row(ROW_CONV_B, 1, a["b_rec_conv"])
            row(ROW_GA_B, 1, a["b_gate_a"])
            row(ROW_GX_B, 1, a["b_gate_x"])
            row(ROW_LAMBDA, 1, a["lru_lambda"])

            def frows(layer, landed):
                act.dma_start(frow[layer][FROW_STATE:FROW_STATE + 16, :],
                              a["state_ffn_conv"][layer].rearrange("s k d -> (s k) d")).then_inc(landed, 16)
                act.dma_start(frow[layer][FROW_W:FROW_W + 3, :], a["w_ffn_conv"][layer]).then_inc(landed, 16)
                act.dma_start(frow[layer][FROW_B:FROW_B + 1, :], a["b_ffn_conv"][layer:layer + 1, :]).then_inc(landed, 16)

            frows(0, f_in)
            frows(1, f1_in)

            act.wait_ge(ones_set, 1)
            for c in range(DC):
                act.wait_ge(x_kept, c + 1)
                if c >= 2:
                    act.wait_ge(ss_done, c - 1)
                nc.scalar.activation(sq[:, c % 2, :], hT[:, c, :], ACT.Square).then_inc(sq_done, 1)
            for s in range(SLOTS):
                hi(s, s, 0, unit_shapes(0)[s])
            norm_root(0)
            norm_hi(0)
            act.wait_ge(prm_ready, 1)
            nc.scalar.activation(spl[:, 1, :], spl[:, 0, :], ACT.Exp, scale=-1.0).then_inc(sp_exp, 1)
            act.dma_start(o["lru_conv_sample"][0, :, 0:2, :], a["state_lru_conv"][0, :, 1:3, :]).then_inc(stored, 16)
            for i in range(2):
                act.dma_start(o["ffn_conv_sample"][i, :, 0, :], a["state_ffn_conv"][i, :, 1, :]).then_inc(stored, 16)

            def exp_scores(h):
                for t in range(2):
                    act.wait_ge(lg_max, 2 * h + t + 1)
                    part = slice(0, P) if t == 0 else slice(P, 384)
                    nc.scalar.activation(lg[:, h % 2, part], lg[:, h % 2, part], ACT.Exp, bias=nmx[:, h % 2, t:t + 1],
                                         accum_out=psum_e[:, h % 2, t:t + 1]).then_inc(p_exp, 1)

            def keep_pT(h):
                act.wait_ge(p_turned, h + 1)
                if h >= 2:
                    act.wait_ge(o_mm, h - 1)
                nc.scalar.copy(pT[:, h % 2, :], A[:, 0:384]).then_inc(p_kept, 1)

            def o_high(h):
                act.wait_ge(o_mm, h + 1)
                nc.scalar.activation(zH[:, h, 0:TP], B[:, 0:TP], ACT.Copy).then_inc(o_hi, 1)

            def keep_kv(n):
                tok, smp = (ktok, ksmp) if n < H else (vtok, vsmp)
                h = n % H
                act.wait_ge(kv_turned, n + 1)
                nc.scalar.copy(tok[:, :, h * P:(h + 1) * P], E[:, 0:TP].rearrange("p (t d) -> p t d", t=2)).then_inc(kv_kept, 1)
                nc.scalar.copy(smp[:, h * P:(h + 1) * P], E[0:NS, TP:TP + P]).then_inc(kv_kept, 1)

            for u in range(4 * R_OUT):
                m = u // 4 + 1
                if u == 5:
                    act.wait_ge(wi_turned, 1)
                    nc.scalar.copy(kitok[:], E[:, 64:192].rearrange("p (t d) -> p t d", t=2)).then_inc(ki_kept, 1)
                    nc.scalar.copy(kismp[:], E[0:NS, 192:256]).then_inc(ki_kept, 1)
                if u == 6:
                    act.wait_ge(idx_mm, 1)
                    for b in range(2):
                        nc.scalar.activation(relu0[:, b::2, :], (C, E)[b][:, b * TP:(b + 1) * TP].rearrange("p (h k) -> p h k", h=2),
                                             ACT.Relu).then_inc(idx_relu, 1)
                    for b in range(2):
                        nc.scalar.activation(relu1[:, b::2, :], AB[:, b, :].rearrange("p (h k) -> p h k", h=2),
                                             ACT.Relu).then_inc(idx_relu, 1)
                if u == 9:
                    act.wait_ge(kx_turned, 1)
                    nc.scalar.copy(kxT[:, :, 0:PAST], AB.rearrange("p b (h k) -> p (b h) k", h=2)).then_inc(kx_kept, 1)
                if u == 10:
                    act.wait_ge(ss_mm, 1)
                    nc.scalar.activation(sR[:], C[0:32, 0:PAST + 1], ACT.Relu).then_inc(ss_relu, 1)
                if 14 <= u < 22:
                    keep_kv(u - 14)
                if u == 14:
                    act.wait_ge(qs_turned, 1)
                    nc.scalar.copy(qsmp[:], AB[0:NS, :, :].rearrange("p b n -> p (b n)")).then_inc(qs_kept, 1)
                if u >= 22:
                    keep_kv(u - 14)
                if u == 26:
                    act.wait_ge(smx_done, 1)
                    nc.scalar.activation(sl[:], sl[:], ACT.Exp).then_inc(sexp_done, 1)
                    nc.scalar.activation(pnew[:], lnew2[:], ACT.Exp).then_inc(sexp_done, 1)
                if u >= 25:
                    exp_scores(u - 25)
                if u >= 26:
                    keep_pT(u - 26)
                if u >= 27:
                    o_high(u - 27)
                hi(u + 4, u % 4, m, unit_shapes(m)[u % 4])
            for t in range(3, H + 2):
                if t < 5:
                    keep_kv(11 + t)
                if t < H:
                    exp_scores(t)
                if t - 1 < H:
                    keep_pT(t - 1)
                o_high(t - 2)
            act.wait_ge(so_done, 1)
            nc.scalar.activation(zH[:, 0:H, TP:T], onw2[:].rearrange("p (h s) -> p h s", h=H), ACT.Copy).then_inc(so_hi, 1)

            def out_rounds(r0, k):
                for n in range(DC):
                    u = 4 * r0 + n
                    m = r0 + n // 4 + 1
                    hi(u + 4, n % 4, m, unit_shapes(m)[n % 4])
                    square(DC * k + n, n % 2, n, u + 1)
                norm_root(k)
                norm_hi(k)

            def up_round(layer, m, i, nxt):
                for p in range(2):
                    s = 2 * p
                    u, j = m * 4 + s, i * 2 + p
                    n = i * 2 + (FC * layer + p)
                    act.wait_ge(unit_done, u + 1)
                    nc.scalar.activation(tails[:, bass.ds(j, 1), 0:10], acc[:, s:s + 1, TP - 2:T], ACT.Copy, scale=INV)
                    nc.scalar.activation(c32[:, p, :], acc[:, s, 0:T], ACT.Identity, scale=fw[layer][:, bass.ds(j, 1), 2:3],
                                         bias=fprm[layer][:, bass.ds(j, 1), FROW_B:FROW_B + 1]).then_inc(conv0, 1)
                    hi(u + 4, s, m + 1, nxt)
                    act.wait_ge(acc_read, u + 1)
                    nc.scalar.activation(c32[:, p, :], c32[:, p, :], ACT.Gelu_apprx_tanh).then_inc(gelu_done, 1)
                    hi(u + 5, s + 1, m + 1, nxt)
                    act.wait_ge(acc_read, u + 2)
                    nc.scalar.activation(zH[:, bass.ds(j, 1), :], z32[:, p:p + 1, :], ACT.Copy).then_inc(z_hi, 1)

            def keep_tails(layer, part):
                act.wait_ge(tail_turned, 2 * layer + part + 1)
                if part == 0:
                    act.wait_ge(kv_stored, 16 * 6)
                ins = None
                for b in range(4 if part == 0 else 2):
                    c0 = 16 * part + 4 * b
                    n = min(4, FC - c0)
                    ins = nc.scalar.copy(rows[0:10, c0 * P:(c0 + n) * P], misc[0:10, b, 0:n * P])
                ins.then_inc(tail_kept, 1)

            def ffn(layer):
                r0 = R_UP[layer]
                with act.Fori(0, UP_ROUNDS - 1) as i:
                    up_round(layer, i + r0, i, (DC, P))
                up_round(layer, r0 + UP_ROUNDS - 1, UP_ROUNDS - 1, (DOWN_HALF, P))
                r0, k = R_DOWN[layer], 2 + 2 * layer
                keep_tails(layer, 0)

                def down_round(m, i, nxt):
                    for p in range(2):
                        u = m * 4 + 2 * p
                        for q in range(2):
                            if nxt:
                                hi(u + 4 + q, 2 * p + q, m + 1, nxt)
                        square(i * 2 + (DC * k + p), p, i * 2 + p, u + 2)

                with act.Fori(0, 3) as i:
                    down_round(i + r0, i, (DOWN_HALF, P))
                down_round(r0 + 3, 3, (DC, P) if layer == 0 else None)
                norm_root(k)
                if k < 4:
                    norm_hi(k)
                keep_tails(layer, 1)

            out_rounds(R_OUT, 1)
            ffn(0)

            for n in range(DC):
                u = 4 * R_XB + n
                act.wait_ge(unit_done, u + 1)
                nc.scalar.activation(tails[:, n, :], acc[:, n % 4, TP - 3:T], ACT.Copy, scale=INV)
                nc.scalar.activation(xc[:, n, :], acc[:, n % 4, 0:T], ACT.Identity, scale=rw[:, n, 3:4],
                                     bias=prm[:, n, ROW_CONV_B:ROW_CONV_B + 1]).then_inc(rc0, 1)
                hi(u + 4, n % 4, R_XB + n // 4 + 1, (DC, P))
                if n == 2:
                    act.wait_ge(g_in, 32)
                    nc.scalar.activation(g_hi[:], gstage[:], ACT.Copy, scale=WSCALE).then_inc(g_hi_done, 1)
                act.wait_ge(acc_read, u + 1)
                nc.scalar.activation(zH[:, DC + n, :], xc[:, n, :], ACT.Copy).then_inc(xc_hi, 1)

            def gate_tanhs_of_sums(n):
                b = 2 * (n % 2)
                act.wait_ge(gate_mm, n + 1)
                if n >= 2:
                    act.wait_ge(ix_done, n - 1)
                    act.wait_ge(gate_tanh, 2 * n - 2)
                for g in range(2):
                    nc.scalar.activation(gates[:, n % 2, g, :], misc[:, b + g, 0:T], ACT.Tanh, scale=INV / 2,
                                         bias=spl[:, 8 + g, n:n + 1]).then_inc(gate_halved, 1)

            def gate_tanhs(n):
                act.wait_ge(gate_sig, n + 1)
                nc.scalar.activation(bq[:, n, :], gates[:, n % 2, 0, :], ACT.Tanh, scale=spl[:, 7, n:n + 1]).then_inc(gate_tanh, 1)
                nc.scalar.activation(decay[:, n, :], gates[:, n % 2, 0, :], ACT.Exp, scale=spl[:, 6, n:n + 1]).then_inc(gate_tanh, 1)

            for n in range(DC):
                u = 4 * R_GATE + n
                hi(u + 4, n % 4, R_GATE + n // 4 + 1, (DC, P))
                gate_tanhs_of_sums(n)
                if n >= 1:
                    gate_tanhs(n - 1)
            gate_tanhs(DC - 1)
            act.wait_ge(gate_tanh, 2 * DC)
            nc.scalar.activation(bq[:], bq[:], ACT.Sqrt).then_inc(b_root, 1)
            act.wait_ge(acc_read, 4 * R_GATE + DC)
            nc.scalar.activation(gateT[:], gateT[:], ACT.Gelu_apprx_tanh).then_inc(ggelu, 1)
            for n in range(DC):
                act.wait_ge(y_full, n + 1)
                nc.scalar.activation(zH[:, n, :], y32[:, n % 2, :], ACT.Copy).then_inc(y_hi, 1)
            act.wait_ge(rt_turned, 1)
            nc.scalar.copy(rrows[:], misc[0:11, 0:2, :].rearrange("p b n -> p (b n)")).then_inc(rt_kept, 1)
            act.wait_ge(rt_turned, 2)
            nc.scalar.copy(hrows[:], misc[0:9, 2:4, :].rearrange("p b n -> p (b n)")).then_inc(rt_kept, 1)
            out_rounds(R_ROUT, 3)
            ffn(1)
            for c in range(DC):
                act.wait_ge(yt_turned, c + 1)
                nc.scalar.copy(ytok[:, :, c * P:(c + 1) * P], misc[:, c % 2, 0:TP].rearrange("p (t d) -> p t d", t=2))
                nc.scalar.copy(ysmp[:, c * P:(c + 1) * P], misc[0:NS, c % 2, TP:TP + P]).then_inc(yt_kept, 1)

        @block.vector
        def _(dve):
            steps = Steps(dve, dve_step)
            v = nc.vector

            def lo(u, s, shape):
                n, cols = shape
                dve.wait_ge(hi_done, u + 1)
                v.scalar_tensor_tensor(w_lo[:, s, 0:n, 0:cols], stage[:, s, 0:n, 0:cols], WSCALE,
                                       w_hi[:, s, 0:n, 0:cols], ALU.mult, ALU.subtract).then_inc(lo_done, 1)

            def norm_apply(k, keep=None):
                dve.wait_ge(rms_root, k + 1)
                steps.done(v.reciprocal(rinv[:], root[:]))
                steps.wait()
                for c in range(DC):
                    dst = keep[:, c, :] if keep is not None else a32[:, c % 2, :]
                    if keep is None and c >= 2:
                        dve.wait_ge(a_lo, DC * k + c - 1)
                    v.scalar_tensor_tensor(dst, hT[:, c, :], prm[:, c, k:k + 1], rinv[:], ALU.mult,
                                           ALU.mult).then_inc(yt_full if keep is not None else a_full, 1)
                    if keep is None and c:
                        norm_lo(k, c - 1)
                if keep is None:
                    norm_lo(k, DC - 1)

            def norm_lo(k, c):
                dve.wait_ge(a_hi, DC * k + c + 1)
                v.tensor_tensor(aL[:, c, :], a32[:, c % 2, :], aH[:, c, :], ALU.subtract).then_inc(a_lo, 1)

            for c in range(DC):
                dve.wait_ge(x_turned, c + 1)
                v.tensor_copy(hT[:, c, :], misc[:, c % 2, 0:T]).then_inc(x_kept, 1)
            dve.wait_ge(prm_turned, 1)
            v.tensor_copy(prm[:], C[:, 0:DC * ROWS_REC].rearrange("p (c r) -> p c r", c=DC)).then_inc(prm_kept, 1)
            dve.wait_ge(prm_kept, 1)
            for s in range(SLOTS):
                lo(s, s, unit_shapes(0)[s])
            norm_apply(0)
            lam = prm[:, :, ROW_LAMBDA]
            steps.done(v.tensor_scalar(spl[:, 2, :], lam, -1.0, None, ALU.mult))
            v.tensor_scalar(spl[:, 8, :], prm[:, :, ROW_GA_B], 0.5, None, ALU.mult)
            v.tensor_scalar(spl[:, 9, :], prm[:, :, ROW_GX_B], 0.5, None, ALU.mult)
            steps.wait()
            v.tensor_tensor(spl[:, 0, :], lam, spl[:, 2, :], ALU.max).then_inc(prm_ready, 1)

            def softplus():
                dve.wait_ge(sp_exp, 1)
                steps.done(v.tensor_scalar(spl[:, 3, :], spl[:, 1, :], 2.0, None, ALU.add)); steps.wait()
                steps.done(v.reciprocal(spl[:, 3, :], spl[:, 3, :])); steps.wait()
                steps.done(v.tensor_tensor(spl[:, 3, :], spl[:, 3, :], spl[:, 1, :], ALU.mult)); steps.wait()
                steps.done(v.tensor_tensor(spl[:, 4, :], spl[:, 3, :], spl[:, 3, :], ALU.mult)); steps.wait()
                steps.done(v.tensor_scalar(spl[:, 5, :], spl[:, 4, :], 1.0 / 17.0, None, ALU.mult)); steps.wait()
                for n in range(15, 2, -2):
                    steps.done(v.scalar_tensor_tensor(spl[:, 5, :], spl[:, 5, :], 1.0 / n, spl[:, 4, :], ALU.add, ALU.mult))
                    steps.wait()
                steps.done(v.scalar_tensor_tensor(spl[:, 5, :], spl[:, 5, :], 1.0, spl[:, 3, :], ALU.add, ALU.mult)); steps.wait()
                steps.done(v.tensor_scalar(spl[:, 10, :], spl[:, 2, :], 0.0, 0.5, ALU.max, ALU.mult)); steps.wait()
                steps.done(v.tensor_tensor(spl[:, 5, :], spl[:, 5, :], spl[:, 10, :], ALU.add)); steps.wait()
                v.tensor_scalar(spl[:, 7, :], spl[:, 5, :], RG_C, None, ALU.mult)
                steps.done(v.tensor_scalar(spl[:, 6, :], spl[:, 5, :], -2.0 * RG_C, None, ALU.mult))

            def rope(u, dst, cos, sin, half, rows_n=P):
                s = u % 4
                dve.wait_ge(unit_done, u + 1)
                if u >= 2:
                    n = min(u, 3) if u < 4 else u - 1
                    dve.wait_ge(roped, n - 1)
                v.tensor_tensor(dst, acc[0:rows_n, s, 0:T], cos[0:rows_n, :], ALU.mult)
                for b in range(0, rows_n, 2 * half):
                    v.tensor_tensor(rot[b:b + half, u % 2, :], acc[b + half:b + 2 * half, s, 0:T],
                                    sin[b + half:b + 2 * half, :], ALU.mult)
                    ins = v.tensor_tensor(rot[b + half:b + 2 * half, u % 2, :], acc[b:b + half, s, 0:T],
                                          sin[b:b + half, :], ALU.mult)
                ins.then_inc(acc_read, 1)

            cosh, sinh = ca[:, CA_COSH:CA_COSH + T], ca[:, CA_SINH:CA_SINH + T]
            cosi, sini = ca[:, CA_COSI:CA_COSI + T], ca[:, CA_SINI:CA_SINI + T]

            def take(work, n):
                for _ in range(n):
                    steps.done(v.max(top8[0:P, :], work)); steps.wait()
                    steps.done(v.match_replace(work, top8[0:P, :], work, TAKEN)); steps.wait()

            def take_sample(r):
                steps.done(v.max(s8[:], sscore[:])); steps.wait()
                v.max_index(i8[:, 8 * r:8 * r + 8], s8[:], sscore[:])
                steps.done(v.match_replace(sscore[:], s8[:], sscore[:], TAKEN)); steps.wait()

            def logits(h):
                dve.wait_ge(lg_mm, h + 1)
                if h == 0:
                    dve.wait_ge(bias_masked, 2)
                if h >= 2:
                    dve.wait_ge(p_turned, h - 1)
                steps.done(v.scalar_tensor_tensor(lg[:, h % 2, :], C[:, 0:384], SCALE, abias[:], ALU.mult, ALU.add))
                steps.wait()
                v.tensor_reduce(nmx[:, h % 2, 0:1], lg[:, h % 2, 0:P], AX.X, ALU.max, negate=True).then_inc(lg_max, 1)
                v.tensor_reduce(nmx[:, h % 2, 1:2], lg[:, h % 2, P:384], AX.X, ALU.max, negate=True).then_inc(lg_max, 1)

            def sums(h):
                dve.wait_ge(p_exp, 2 * h + 2)
                v.reciprocal(prcp[:, h % 2, :], psum_e[:, h % 2, :]).then_inc(p_rcp, 1)

            def o_low(h):
                dve.wait_ge(o_hi, h + 1)
                v.tensor_tensor(zL[:, h, 0:TP], B[:, 0:TP], zH[:, h, 0:TP], ALU.subtract).then_inc(o_lo, 1)

            def sample_dots(j):
                dve.wait_ge(qb_mm, j + 1)
                dve.wait_ge(kg_in[j], 16)
                steps.done(v.tensor_tensor(prod[:].rearrange("p (b n) -> p b n", b=2), AB,
                                kgat[:, j, :].rearrange("p (b n) -> p b n", b=2), ALU.mult)); steps.wait()
                v.sem_inc(qb_read, 1) if False else None
                steps.done(v.tensor_reduce(qk[:, j, :], prod[:].rearrange("p (h d) -> p h d", h=H), AX.X, ALU.add))
                steps.wait()
                v.tensor_scalar(qkb[:, j, :], qk[:, j, :], SCALE, gbias[:, j:j + 1], ALU.mult, ALU.add).then_inc(qb_read, 1)

            def small(ins):
                steps.done(ins); steps.wait()

            def keep_fprm(layer):
                dve.wait_ge(fprm_turned, layer + 1)
                v.tensor_copy(fprm[layer][:], (A if layer == 0 else B)[:, 0:FC * ROWS_FFN].rearrange("p (c r) -> p c r", c=FC)
                              ).then_inc(fprm_kept, 1)

            for u in range(4 * R_OUT):
                if u in (2, 3):
                    keep_fprm(u - 2)
                if u == 3:
                    dve.wait_ge(roped, 3)
                    v.tensor_copy(kiT[ID:P, :], kiT[0:ID, :]).then_inc(ki_twice, 1)
                    dve.wait_ge(qz_zero, 1)
                    for half in range(2):
                        rows_ = slice(ID * half, ID * half + ID)
                        for ih in range(IH):
                            src = qiT[ID * (ih % 2):ID * (ih % 2) + ID, ih // 2, TP + half:T:2]
                            off = 4 * half + ih
                            dst = qz[rows_].rearrange("p j n -> p (j n)")[:, off:off + 121:40]
                            v.tensor_copy(dst, src)
                        ins = v.tensor_copy(kxT[rows_, :, PAST], kiT[0:ID, TP + half:T:2])
                    ins.then_inc(qz_done, 1)
                if u == 6:
                    softplus()
                if u == 5:
                    dve.wait_ge(ki_kept, 2)
                    v.tensor_scalar(wtok[:], E[:, 0:8].rearrange("p (t h) -> p t h", t=2), IDX_SCALE * INV, None,
                                    ALU.mult).then_inc(wtok_done, 1)
                if u == 6:
                    dve.wait_ge(wtok_done, 1)
                    for t, (rel, part) in enumerate(((relu0, score[:, 0:P]), (relu1, score[:, P:384]))):
                        dve.wait_ge(idx_relu, 2 * t + 2)
                        small(v.tensor_scalar(part, rel[:, 0, :], wtok[:, t, 0:1], None, ALU.mult))
                        for ih in range(1, IH):
                            ins = v.scalar_tensor_tensor(part, rel[:, ih, :], wtok[:, t, ih:ih + 1], part, ALU.mult, ALU.add)
                            if ih < IH - 1:
                                small(ins)
                        ins.then_inc(idx_sum, 1)
                if u in (7, 8):
                    if u == 7:
                        dve.wait_ge(idx_masked, 1)
                    take(score[:, 0:P], 4)
                if u == 8:
                    v.tensor_scalar(abias[:, 0:P], score[:, 0:P], TAKEN, OUT_OF_REACH, ALU.not_equal, ALU.mult).then_inc(bias_done, 1)
                if u == 9:
                    dve.wait_ge(wrep_mm, 1)
                    v.scalar_tensor_tensor(wblk[:], C[0:32, 384:392], IDX_SCALE * INV, cb[0:32, CB_SAME:CB_SAME + NS],
                                           ALU.mult, ALU.mult).then_inc(wblk_done, 1)
                if 9 <= u < 13:
                    if u == 9:
                        dve.wait_ge(idx_masked, 2)
                    take(score[:, P:384], 2)
                if u == 12:
                    v.tensor_scalar(abias[:, P:384], score[:, P:384], TAKEN, OUT_OF_REACH, ALU.not_equal, ALU.mult).then_inc(bias_done, 1)
                if u == 13:
                    dve.wait_ge(sc_mm, 1)
                    v.tensor_copy(sscore[:], B[0:NS, 0:PAST + 1]).then_inc(sscore_kept, 1)
                    dve.wait_ge(sscore_kept, 1)
                if 13 <= u < 17:
                    take_sample(2 * (u - 13))
                    take_sample(2 * (u - 13) + 1)
                if u == 16:
                    dve.wait_ge(pt_in, 32)
                    small(v.tensor_copy(idxf[:], i8[:]))
                    small(v.tensor_scalar(pt8f[:, 0:2], pt8[:], float(PAGE), None, ALU.mult))
                    small(v.tensor_tensor(pt8f[:, 2:3], pt8f[:, 1:2], pt8f[:, 0:1], ALU.subtract))
                    small(v.tensor_scalar(pt8f[:, 3:4], pt8f[:, 2:3], -float(PAGE), None, ALU.add))
                    for r in range(2):
                        v.tensor_scalar(flag2[:, 64 * r:64 * r + 64], idxf[:], float(PAST), OUT_OF_REACH, ALU.is_equal, ALU.mult)
                    small(v.tensor_scalar(idxt[:], idxf[:], float(PAST), None, ALU.is_equal))
                    small(v.tensor_reduce(selnew[:, 0:1], idxt[:], AX.X, ALU.max))
                    small(v.tensor_scalar(selnew[:, 1:2], selnew[:, 0:1], -1.0, -OUT_OF_REACH, ALU.add, ALU.mult))
                    small(v.tensor_scalar(seld[:], ident[0:NS, 0:NS], selnew[:, 1:2], None, ALU.mult))
                    small(v.tensor_scalar(idxf[:], idxf[:], float(PAST - 1), None, ALU.min))
                    small(v.tensor_scalar(idxt[:], idxf[:], float(PAGE), pt8f[:, 3:4], ALU.is_ge, ALU.mult))
                    v.scalar_tensor_tensor(phys2[:, 0:64], idxf[:], pt8f[:, 0:1], idxt[:], ALU.add, ALU.add)
                    v.scalar_tensor_tensor(phys2[:, 64:128], idxf[:], pt8f[:, 0:1], idxt[:], ALU.add, ALU.add).then_inc(phys_done, 1)
                if u == 18:
                    dve.wait_ge(phys_turned, 1)
                    for half in range(2):
                        r = slice(64 * half, 64 * half + 64)
                        v.tensor_copy(gbias[r, :], C[r, 8 + half:16:2])
                        ins = v.tensor_copy(gix[r, :], C[r, half:8:2])
                        ins.then_inc(gix_done, 1)
                if u == 20:
                    dve.wait_ge(roped, 3 + 2 * H)
                    v.tensor_tensor(nprod[:].rearrange("p (h s) -> p h s", h=H), qT[:, :, TP:T], kT[:, :, TP:T],
                                    ALU.mult).then_inc(nprod_done, 1)
                    sample_dots(0)
                if 21 <= u < 24:
                    sample_dots(u - 20)
                if u == 25:
                    dve.wait_ge(sl_turned, 1)
                    steps.done(v.tensor_tensor(nl[:].rearrange("p (h s) -> p h s", h=H),
                                    B[0:NS, 0:64].rearrange("p (h s) -> p h s", h=H),
                                    cb[0:NS, CB_HEAD:CB_HEAD + 64].rearrange("p (h s) -> p h s", h=H), ALU.mult)); steps.wait()
                    small(v.tensor_reduce(lnew[:], nl[:].rearrange("p (h s) -> p s h", h=H), AX.X, ALU.add))
                    small(v.scalar_tensor_tensor(lnew[:], lnew[:], SCALE, B[0:NS, 64:72], ALU.mult, ALU.add))
                    small(v.tensor_reduce(smx[:], A[0:NS, :].rearrange("p (s k) -> p s k", s=NS), AX.X, ALU.max))
                    small(v.tensor_tensor(smx[:], smx[:], lnew[:], ALU.max))
                    v.tensor_tensor(lnew2[:], lnew[:], smx[:], ALU.subtract)
                    v.tensor_tensor(sl[:].rearrange("p (s k) -> p s k", s=NS), A[0:NS, :].rearrange("p (s k) -> p s k", s=NS),
                                    smx[:].unsqueeze(2).to_broadcast([NS, NS, TOPK]), ALU.subtract).then_inc(smx_done, 1)
                if u == 27:
                    dve.wait_ge(sexp_done, 2)
                    small(v.tensor_reduce(ssum[:], sl[:].rearrange("p (s k) -> p s k", s=NS), AX.X, ALU.add))
                    small(v.tensor_tensor(ssum[:], ssum[:], pnew[:], ALU.add))
                    small(v.reciprocal(ssum[:], ssum[:]))
                    small(v.tensor_tensor(pnew[:], pnew[:], ssum[:], ALU.mult))
                    v.tensor_tensor(pnd[:].rearrange("p (h s) -> p h s", h=H),
                                    cb[0:NS, CB_HEAD:CB_HEAD + 64].rearrange("p (h s) -> p h s", h=H),
                                    pnew[:].unsqueeze(1).to_broadcast([NS, H, NS]), ALU.mult)
                    v.tensor_tensor(sl[:].rearrange("p (s k) -> p s k", s=NS), sl[:].rearrange("p (s k) -> p s k", s=NS),
                                    ssum[:].unsqueeze(2).to_broadcast([NS, NS, TOPK]), ALU.mult).then_inc(sp_done, 1)
                if u >= 25:
                    logits(u - 25)
                if u >= 26:
                    sums(u - 26)
                if u >= 27:
                    o_low(u - 27) if u > 27 else None
                h = (u - 4) % 8
                if u < 2:
                    rope(u, qiT[:, u, :], cosi, sini, ID // 2)
                elif u == 2:
                    rope(u, kiT[0:ID, :], cosi, sini, ID // 2, ID)
                elif u == 3:
                    dve.wait_ge(unit_done, u + 1)
                    v.tensor_copy(wiT[:], acc[0:IH, 3, 0:T]).then_inc(acc_read, 1)
                elif u < 4 * R_K:
                    rope(u, qT[:, h, :], cosh, sinh, P // 2)
                elif u < 4 * R_V:
                    rope(u, kT[:, h, :], cosh, sinh, P // 2)
                else:
                    dve.wait_ge(unit_done, u + 1)
                    if h >= 2:
                        dve.wait_ge(kv_turned, H + h - 1)
                    v.tensor_scalar(vnew[:, h, :], acc[:, u % 4, TP:T], INV, None, ALU.mult)
                    v.tensor_scalar(vT[:, h % 2, :], acc[:, u % 4, 0:T], INV, None, ALU.mult).then_inc(acc_read, 1)
                lo(u + 4, u % 4, unit_shapes(u // 4 + 1)[u % 4])
            for t in range(3, H + 3):
                if t < H:
                    logits(t)
                if t - 1 < H:
                    sums(t - 1)
                if t - 3 < H:
                    o_low(t - 3)
            dve.wait_ge(sp_turned, 1)
            dve.wait_ge(qz_zero, 2)
            for half in range(2):
                r = slice(64 * half, 64 * half + 64)
                ins = v.tensor_copy(pb[r, :, :, half], E[r, 0:32].rearrange("p (j h) -> p j h", j=4))
            ins.then_inc(pb_done, 1)
            dve.wait_ge(so_mm, 1)
            small(v.tensor_tensor(onew[:], E[:, 128:192], vnew[:].rearrange("p h s -> p (h s)"), ALU.mult))
            v.tensor_tensor(onw2[:], E[:, 64:128], onew[:], ALU.add).then_inc(so_done, 1)
            dve.wait_ge(so_hi, 1)
            dve.wait_ge(so_done, 1)
            v.tensor_tensor(zL[:, 0:H, TP:T], onw2[:].rearrange("p (h s) -> p h s", h=H), zH[:, 0:H, TP:T],
                            ALU.subtract).then_inc(o_lo, 1)

            def out_rounds(r0, k):
                for n in range(DC):
                    u = 4 * r0 + n
                    dve.wait_ge(unit_done, u + 1)
                    if n < 2 and False:
                        pass
                    v.scalar_tensor_tensor(hT[:, n, :], acc[:, n % 4, 0:T], INV, hT[:, n, :], ALU.mult, ALU.add).then_inc(acc_read, 1)
                    lo(u + 4, n % 4, unit_shapes(r0 + n // 4 + 1)[n % 4])
                norm_apply(k)

            def up_round(layer, m, i, nxt, own):
                for p in range(2):
                    s = 2 * p
                    u, j = m * 4 + s, i * 2 + p
                    n = i * 2 + (FC * layer + p)
                    tap = fw[layer]
                    dve.wait_ge(conv0, n + 1)
                    v.scalar_tensor_tensor(c32[:, p, 1:TP], acc[:, s, 0:TP - 1], tap[:, bass.ds(j, 1), 1:2], c32[:, p, 1:TP],
                                           ALU.mult, ALU.add).then_inc(dve_step, 1)
                    v.tensor_tensor(c32[:, p:p + 1, TP:T], c32[:, p:p + 1, TP:T], fpre[layer][:, bass.ds(j, 1), :], ALU.add)
                    dve.wait_ge(dve_step, own + (p + 1))
                    v.scalar_tensor_tensor(c32[:, p, 2:TP], acc[:, s, 0:TP - 2], tap[:, bass.ds(j, 1), 0:1], c32[:, p, 2:TP],
                                           ALU.mult, ALU.add).then_inc(acc_read, 1)
                    lo(u + 4, s, nxt)
                    dve.wait_ge(gelu_done, n + 1)
                    dve.wait_ge(unit_done, u + 2)
                    v.scalar_tensor_tensor(z32[:, p, :], acc[:, s + 1, 0:T], INV, c32[:, p, :], ALU.mult, ALU.mult).then_inc(acc_read, 1)
                    lo(u + 5, s + 1, nxt)
                    dve.wait_ge(z_hi, n + 1)
                    v.tensor_tensor(zL[:, bass.ds(j, 1), :], z32[:, p:p + 1, :], zH[:, bass.ds(j, 1), :], ALU.subtract).then_inc(z_lo, 1)

            def down_round(m, i, nxt):
                for p in range(2):
                    u = m * 4 + 2 * p
                    dve.wait_ge(unit_done, u + 2)
                    chunk = hT[:, bass.ds(i * 2 + p, 1), :]
                    v.scalar_tensor_tensor(chunk, acc[:, 2 * p:2 * p + 1, 0:T], INV, chunk, ALU.mult, ALU.add).then_inc(acc_read, 2)
                    if nxt:
                        lo(u + 4, 2 * p, nxt)
                        lo(u + 5, 2 * p + 1, nxt)

            def ffn(layer):
                r0, own = R_UP[layer], steps.n
                with dve.Fori(0, UP_ROUNDS - 1) as i:
                    up_round(layer, i + r0, i, (DC, P), i * 2 + own)
                steps.n = own + 2 * (UP_ROUNDS - 1)
                up_round(layer, r0 + UP_ROUNDS - 1, UP_ROUNDS - 1, (DOWN_HALF, P), steps.n)
                steps.n += 2
                r0, k = R_DOWN[layer], 2 + 2 * layer
                with dve.Fori(0, 3) as i:
                    down_round(i + r0, i, (DOWN_HALF, P))
                down_round(r0 + 3, 3, (DC, P) if layer == 0 else None)
                norm_apply(k, yT if k == 4 else None)

            out_rounds(R_OUT, 1)
            dve.wait_ge(prm_ready, 3)
            ffn(0)

            for n in range(DC):
                u, s = 4 * R_XB + n, n % 4
                dve.wait_ge(rc0, n + 1)
                for k in (1, 2, 3):
                    ins = v.scalar_tensor_tensor(xc[:, n, k:TP], acc[:, s, 0:TP - k], rw[:, n, 3 - k:4 - k], xc[:, n, k:TP],
                                                 ALU.mult, ALU.add)
                    if k == 1:
                        v_s = v.tensor_tensor(xc[:, n, TP:T], xc[:, n, TP:T], rpre[:, n, :], ALU.add)
                    if k < 3:
                        steps.done(ins if k > 1 else v_s); steps.wait()
                ins.then_inc(acc_read, 1)
                lo(u + 4, s, (DC, P))
                if n == 2:
                    dve.wait_ge(g_hi_done, 1)
                    v.scalar_tensor_tensor(g_lo[:], gstage[:], WSCALE, g_hi[:], ALU.mult, ALU.subtract).then_inc(g_lo_done, 1)
                dve.wait_ge(xc_hi, n + 1)
                v.tensor_tensor(zL[:, DC + n, :], xc[:, n, :], zH[:, DC + n, :], ALU.subtract).then_inc(xc_lo, 1)

            def sigmoids(n):
                dve.wait_ge(gate_halved, 2 * n + 2)
                g = gates[:, n % 2]
                v.tensor_scalar(g, g, 0.5, 0.5, ALU.mult, ALU.add).then_inc(gate_sig, 1)

            def b_part(n):
                dve.wait_ge(gate_tanh, 2 * n + 2)
                dve.wait_ge(ix_done, n + 1)
                v.scalar_tensor_tensor(ix[:, n, :], decay[:, n, :], 1.0, ix[:, n, :], ALU.add, ALU.mult).then_inc(bq_done, 1)

            for n in range(DC):
                u, s = 4 * R_GATE + n, n % 4
                dve.wait_ge(unit_done, u + 1)
                v.tensor_scalar(gateT[:, n, :], acc[:, s, 0:T], INV, None, ALU.mult).then_inc(acc_read, 1)
                lo(u + 4, s, (DC, P))
                sigmoids(n)
                if n >= 1:
                    b_part(n - 1)
            b_part(DC - 1)
            dve.wait_ge(b_root, 1)
            dve.wait_ge(bq_done, DC)
            dve.wait_ge(f_stored, 32)
            small(v.tensor_tensor(bq[:], bq[:], ix[:], ALU.mult))
            for n in range(DC):
                v.tensor_tensor_scan(hsT[:, n, 0:TP], decay[:, n, 0:TP], bq[:, n, 0:TP], 0.0, ALU.mult, ALU.add)
            small(v.tensor_tensor(rtmp[:], decay[:, :, TP:T], prm[:, :, ROW_H0:ROW_H0 + NS], ALU.mult))
            v.tensor_tensor(hsT[:, :, TP:T], rtmp[:], bq[:, :, TP:T], ALU.add).then_inc(hs_done, 1)
            dve.wait_ge(hs_done, 1)
            dve.wait_ge(ggelu, 1)
            for n in range(DC + 1):
                if 2 <= n < DC:
                    dve.wait_ge(y_lo, n - 1)
                if n < DC:
                    v.tensor_tensor(y32[:, n % 2, :], gateT[:, n, :], hsT[:, n, :], ALU.mult).then_inc(y_full, 1)
                if n:
                    dve.wait_ge(y_hi, n)
                    v.tensor_tensor(zL[:, n - 1, :], y32[:, (n - 1) % 2, :], zH[:, n - 1, :], ALU.subtract).then_inc(y_lo, 1)
            out_rounds(R_ROUT, 3)
            ffn(1)

        @block.tensor
        def _(pe):
            t_ = nc.tensor

            def unit(u, s, n, xH, xL, cols=P, bank=None, first=True, last=True, x0=0, ready=None):
                bank = s if bank is None else bank
                pe.wait_ge(lo_done, u + 1)
                if first and not (isinstance(u, int) and u < SLOTS):
                    pe.wait_ge(acc_read, u - SLOTS + 1)
                out = acc[0:cols, bank, 0:T]
                for c in range(n):
                    if ready:
                        ready(c)
                    t_.matmul(out, w_hi[:, s, c, 0:cols], xH[:, x0 + c, :], start=first and c == 0, stop=False)
                    t_.matmul(out, w_hi[:, s, c, 0:cols], xL[:, x0 + c, :], start=False, stop=False)
                    ins = t_.matmul(out, w_lo[:, s, c, 0:cols], xH[:, x0 + c, :], start=False, stop=last and c == n - 1)
                ins.then_inc(unit_done, 1)

            def norm_sum(k):
                pe.wait_ge(ss_done, DC * (k + 1))
                t_.matmul(E[:, 0:T], ones[:], sqsum[:], start=True, stop=True).then_inc(rms_sum, 1)

            def a_ready(k):
                return lambda c: pe.wait_ge(a_lo, DC * k + c + 1)

            pe.wait_ge(const_in, 16)
            pe.wait_ge(x0_in, 16)
            pe.wait_ge(x_in, 16)
            pe.wait_ge(xs_in, 32)
            for c in range(DC):
                if c >= 2:
                    pe.wait_ge(x_kept, c - 1)
                cols = slice(c * P, (c + 1) * P)
                t_.transpose(misc[:, c % 2, 0:P], xtok[:, 0, cols], ident)
                t_.transpose(misc[:, c % 2, P:TP], xtok[:, 1, cols], ident)
                t_.transpose(misc[:, c % 2, TP:T], xsmp[:, cols], ident[0:NS, 0:NS]).then_inc(x_turned, 1)
            pe.wait_ge(prm_in, 16 * 12)
            for c in range(DC):
                ins = t_.transpose(C[:, c * ROWS_REC:(c + 1) * ROWS_REC], rowsR[:, c, :], ident[0:ROWS_REC, 0:ROWS_REC])
            ins.then_inc(prm_turned, 1)
            pe.wait_ge(ones_set, 1)
            norm_sum(0)

            def turn_kv(n):
                h = n % H
                if n < H:
                    pe.wait_ge(roped, 3 + H + n + 1)
                else:
                    pe.wait_ge(acc_read, 4 * R_V + h + 1)
                if n:
                    pe.wait_ge(kv_kept, 2 * n)
                src = kT[:, h, :] if n < H else vT[:, h % 2, :]
                t_.transpose(E[:, 0:P], src[:, 0:P], ident)
                t_.transpose(E[:, P:TP], src[:, P:TP], ident)
                t_.transpose(E[0:NS, TP:TP + P], src[:, TP:T], ident).then_inc(kv_turned, 1)

            def head_logits(h):
                if h:
                    pe.wait_ge(lg_max, 2 * h)
                else:
                    pe.wait_ge(gix_done, 2)
                t_.matmul(C[:, 0:P], qT[:, h, 0:P], kT[:, h, 0:P], start=True, stop=True)
                t_.matmul(C[:, P:384], qT[:, h, P:TP], kT[:, h, 0:TP], start=True, stop=True).then_inc(lg_mm, 1)

            def turn_p(h):
                pe.wait_ge(p_norm, 2 * h + 2)
                if h:
                    pe.wait_ge(p_kept, h)
                else:
                    pe.wait_ge(smx_done, 1)
                t_.transpose(A[:, 0:P], lg[:, h % 2, 0:P], ident)
                t_.transpose(A[:, P:TP], lg[:, h % 2, P:TP], ident)
                t_.transpose(A[:, TP:384], lg[:, h % 2, TP:384], ident).then_inc(p_turned, 1)

            def head_out(h):
                pe.wait_ge(p_kept, h + 1)
                pe.wait_ge(kv_kept, 2 * (H + h) + 2)
                if h:
                    pe.wait_ge(o_lo, h)
                hc = slice(h * P, (h + 1) * P)
                t_.matmul(B[:, 0:TP], vtok[:, 0, hc], pT[:, h % 2, 0:TP], start=True, stop=False)
                t_.matmul(B[:, P:TP], vtok[:, 1, hc], pT[:, h % 2, TP:384], start=False, stop=True).then_inc(o_mm, 1)

            for u in range(4 * R_OUT):
                n, cols = unit_shapes(u // 4)[u % 4]
                unit(u, u % 4, n, aH, aL, cols, ready=a_ready(0) if u == 0 else None)
                if u in (1, 2):
                    layer = u - 1
                    pe.wait_ge((f_in, f1_in)[layer], 48)
                    for c in range(FC):
                        ins = t_.transpose((A, B)[layer][:, c * ROWS_FFN:(c + 1) * ROWS_FFN], frow[layer][:, c * P:(c + 1) * P],
                                           ident[0:ROWS_FFN, 0:ROWS_FFN])
                    ins.then_inc(fprm_turned, 1)
                if u == 4:
                    pe.wait_ge(roped, 3)
                    pe.wait_ge(acc_read, 4)
                    for t in range(2):
                        t_.transpose(E[:, 4 * t:4 * t + 4], wiT[:, t * P:(t + 1) * P], ident[0:IH, 0:IH])
                        t_.transpose(E[:, 64 + ID * t:64 + ID * t + ID], kiT[0:ID, t * P:(t + 1) * P], ident[0:ID, 0:ID])
                    t_.transpose(E[0:NS, 192:256], kiT[0:ID, TP:T], ident[0:ID, 0:ID]).then_inc(wi_turned, 1)
                if u == 5:
                    pe.wait_ge(ki_twice, 1)
                    pe.wait_ge(ki_kept, 2)
                    pe.wait_ge(wtok_done, 1)
                    pe.wait_ge(fprm_kept, 2)
                    for ih in range(IH):
                        r = slice(ID * (ih % 2), ID * (ih % 2) + ID)
                        at = ih // 2 * P + ih % 2 * TP
                        t_.matmul((C, E)[ih % 2][:, at:at + P], qiT[r, ih // 2, 0:P], kiT[r, 0:P], start=True, stop=True)
                        ins = t_.matmul(AB[:, ih % 2, (ih // 2) * TP:(ih // 2 + 1) * TP], qiT[r, ih // 2, P:TP], kiT[r, 0:TP],
                                        start=True, stop=True)
                    ins.then_inc(idx_mm, 1)
                if u == 8:
                    pe.wait_ge(idx_relu, 4)
                    for g in range(2):
                        pe.wait_ge(kx_in[g], 16 * NS)
                    for j in range(4):
                        for g in range(2):
                            ins = t_.transpose(AB[:, j // 2, (j % 2) * TP + g * P:(j % 2) * TP + (g + 1) * P],
                                               kx[:, g, j * P:(j + 1) * P], ident)
                    ins.then_inc(kx_turned, 1)
                    pe.wait_ge(xs_in, 32)
                    t_.matmul(C[0:32, 384:392], cb[0:IH, CB_REP:CB_REP + 32], wiT[:, TP:T], start=True, stop=True).then_inc(wrep_mm, 1)
                if u == 9:
                    pe.wait_ge(kx_kept, 1)
                    pe.wait_ge(qz_done, 1)
                    pe.wait_ge(wblk_done, 1)
                    for j in range(4):
                        ins = t_.matmul(C[0:32, 0:PAST + 1], qz[:, j, :], kxT[:, j, :], start=j == 0, stop=j == 3)
                    ins.then_inc(ss_mm, 1)
                if u == 10:
                    pe.wait_ge(ss_relu, 1)
                    t_.matmul(B[0:NS, 0:PAST + 1], wblk[:], sR[:], start=True, stop=True).then_inc(sc_mm, 1)
                if 13 <= u < 21:
                    turn_kv(u - 13)
                if u == 13:
                    pe.wait_ge(roped, 3 + H)
                    for h in range(H):
                        if h == 4:
                            pe.wait_ge(sscore_kept, 1)
                        ins = t_.transpose(AB[0:NS, h // 4, (h % 4) * P:(h % 4 + 1) * P], qT[:, h, TP:T], ident)
                    ins.then_inc(qs_turned, 1)
                if u == 17:
                    pe.wait_ge(phys_done, 1)
                    t_.transpose(C[:, 0:8], phys2[:], ident[0:NS, 0:NS])
                    t_.transpose(C[:, 8:16], flag2[:], ident[0:NS, 0:NS]).then_inc(phys_turned, 1)
                if 19 <= u < 23:
                    j = u - 19
                    pe.wait_ge(qs_kept, 1)
                    if j:
                        pe.wait_ge(qb_read, j)
                    for b in range(2):
                        ins = t_.matmul(AB[:, b, :], cb[0:NS, CB_PAIR + j * P:CB_PAIR + (j + 1) * P], qsmp[:, b * 512:(b + 1) * 512],
                                        start=True, stop=True)
                    ins.then_inc(qb_mm, 1)
                if u == 24:
                    pe.wait_ge(qb_read, 4)
                    pe.wait_ge(nprod_done, 1)
                    for j in range(4):
                        t_.transpose(A[0:NS, j * P:(j + 1) * P], qkb[:, j, :], ident)
                    t_.matmul(B[0:NS, 0:64], ones[:, 0:NS], nprod[:], start=True, stop=True)
                    t_.matmul(B[0:NS, 64:72], ones[0:NS, 0:NS], seld[:], start=True, stop=True).then_inc(sl_turned, 1)
                if u >= 21:
                    turn_kv(u - 13)
                if u >= 24:
                    head_logits(u - 24)
                if u >= 26:
                    turn_p(u - 26)
            head_out(0)
            turn_kv(15)
            for t in range(4, H + 3):
                if t < H:
                    head_logits(t)
                if t - 2 < H:
                    turn_p(t - 2)
                if t - 3 < H:
                    head_out(t - 3)
            pe.wait_ge(sp_done, 1)
            pe.wait_ge(kv_kept, 4 * H)
            for j in range(4):
                ins = t_.transpose(E[:, 8 * j:8 * j + 8], sl[:, j * P:(j + 1) * P], ident[0:NS, 0:NS])
            ins.then_inc(sp_turned, 1)
            pe.wait_ge(pb_done, 1)
            t_.matmul(E[:, 128:192], ones[0:NS, :], pnd[:], start=True, stop=True)
            for j in range(4):
                pe.wait_ge(vg_in[j], 16)
                for h in range(H):
                    ins = t_.matmul(E[:, 64 + 8 * h + 2 * j:64 + 8 * h + 2 * j + 2], vgat[:, j, h * P:(h + 1) * P], pb[:, j, h, :],
                                    start=True, stop=True)
            ins.then_inc(so_mm, 1)

            def out_rounds(r0, k, ready):
                for n in range(DC):
                    u = 4 * r0 + n
                    unit(u, n % 4, DC, zH, zL, ready=ready if n == 0 else None)
                norm_sum(k)

            def o_ready(c):
                pe.wait_ge(o_lo, H + 1)

            def turn_tails(layer, part):
                if part == 1:
                    pe.wait_ge(tail_kept, 2 * layer + 1)
                for c in range(16 * part, 16 if part == 0 else FC):
                    b = (c - 16 * part) // 4
                    ins = t_.transpose(misc[0:10, b, (c % 4) * P:(c % 4 + 1) * P], tails[:, c, 0:10], ident)
                ins.then_inc(tail_turned, 1)

            def ffn(layer, k):
                r0 = R_UP[layer]
                with pe.Fori(0, UP_ROUNDS) as i:
                    for s in range(SLOTS):
                        unit(i * 4 + (4 * r0 + s), s, DC, aH, aL, ready=a_ready(k) if s == 0 else None)
                pe.wait_ge(conv0, FC * (layer + 1))
                if layer == 0:
                    pe.wait_ge(rms_root, k + 1)
                turn_tails(layer, 0)
                r0 = R_DOWN[layer]
                with pe.Fori(0, 4) as i:
                    for s in range(SLOTS):
                        half = s % 2
                        u = i * 4 + (4 * r0 + s)
                        unit(u, s, DOWN_HALF, zH, zL, bank=2 * (s // 2), first=half == 0, last=half == 1, x0=half * DOWN_HALF,
                             ready=(lambda c, half=half: pe.wait_ge(z_lo, FC * layer + half * DOWN_HALF + c + 1)) if s < 2 else None)
                pe.wait_ge(tail_kept, 2 * layer + 1)
                norm_sum(k + 1)
                turn_tails(layer, 1)

            out_rounds(R_OUT, 1, o_ready)
            ffn(0, 1)
            for n in range(DC):
                unit(4 * R_XB + n, n % 4, DC, aH, aL, ready=a_ready(2) if n == 0 else None)
            for n in range(DC):
                unit(4 * R_GATE + n, n % 4, DC, aH, aL)
                pe.wait_ge(xc_lo, n + 1)
                if n == 0:
                    pe.wait_ge(g_lo_done, 1)
                    pe.wait_ge(tail_kept, 2)
                    pe.wait_ge(rms_root, 3)
                if n >= 2:
                    pe.wait_ge(gate_halved, 2 * n - 2)
                for g in range(2):
                    out = misc[:, 2 * (n % 2) + g, 0:T]
                    t_.matmul(out, g_hi[:, g, n, :], zH[:, DC + n, :], start=True, stop=False)
                    t_.matmul(out, g_hi[:, g, n, :], zL[:, DC + n, :], start=False, stop=False)
                    ins = t_.matmul(out, g_lo[:, g, n, :], zH[:, DC + n, :], start=False, stop=True)
                ins.then_inc(gate_mm, 1)
            pe.wait_ge(gate_halved, 2 * DC)
            for c in range(DC):
                ins = t_.transpose(misc[0:11, c // 4, (c % 4) * P:(c % 4 + 1) * P], tails[:, c, :], ident)
            ins.then_inc(rt_turned, 1)
            pe.wait_ge(hs_done, 1)
            for c in range(DC):
                ins = t_.transpose(misc[0:9, 2 + c // 4, (c % 4) * P:(c % 4 + 1) * P], hsT[:, c, TP - 1:T], ident)
            ins.then_inc(rt_turned, 1)
            for n in range(DC):
                unit(4 * R_ROUT + n, n % 4, DC, zH, zL, ready=(lambda c: pe.wait_ge(y_lo, c + 1)) if n == 0 else None)
            pe.wait_ge(rt_kept, 2)
            norm_sum(3)
            ffn(1, 3)
            for c in range(DC):
                pe.wait_ge(yt_full, c + 1)
                if c == 0:
                    pe.wait_ge(tail_kept, 4)
                if c >= 2:
                    pe.wait_ge(yt_kept, c - 1)
                t_.transpose(misc[:, c % 2, 0:P], yT[:, c, 0:P], ident)
                t_.transpose(misc[:, c % 2, P:TP], yT[:, c, P:TP], ident)
                t_.transpose(misc[0:NS, c % 2, TP:TP + P], yT[:, c, TP:T], ident).then_inc(yt_turned, 1)

        @block.gpsimd
        def _(pool):
            g = nc.gpsimd
            steps = Steps(pool, pool_step)

            def small(ins):
                steps.done(ins)
                steps.wait()

            def add_square(n, p, first):
                pool.wait_ge(sq_done, n + 1)
                if first:
                    if not (isinstance(n, int) and n == 0):
                        pool.wait_ge(rms_sum, first)
                    g.tensor_copy(sqsum[:], sq[:, p, :]).then_inc(ss_done, 1)
                else:
                    pool.wait_ge(ss_done, n)
                    g.tensor_tensor(sqsum[:], sqsum[:], sq[:, p, :], ALU.add).then_inc(ss_done, 1)

            def add_squares(k):
                for c in range(DC):
                    add_square(DC * k + c, c % 2, k if c == 0 and k else (True if c == 0 else False))

            g.memset(ones[:], 1.0)
            g.memset(epsc[:], EPS).then_inc(ones_set, 1)
            add_squares(0)
            g.memset(qz[:], 0.0).then_inc(qz_zero, 1)
            g.memset(pb[:], 0.0).then_inc(qz_zero, 1)
            pool.wait_ge(pt_in, 32)
            pool.wait_ge(const_in, 16)
            g.tensor_scalar(gidx[:], ptb[:], float(PAGE), ca[:, CA_IOTA:CA_IOTA + 1], ALU.mult, ALU.add).then_inc(gidx_done, 1)
            pool.wait_ge(gidx_done, 1)
            kidx_rows = a["cache_kidx"].rearrange("a n p d -> (a n p) d")
            for s in range(NS):
                for page in range(2):
                    g.indirect_dma_start(out=kx[:, page, s * ID:(s + 1) * ID], out_offset=None, in_=kidx_rows,
                                         in_offset=bass.IndirectOffsetOnAxis(ap=gidx[:, 2 * s + page:2 * s + page + 1], axis=0)
                                         ).then_inc(kx_in[page], 16)

            def conv_params():
                pool.wait_ge(prm_kept, 1)
                g.tensor_scalar(rw[:], prm[:, :, ROW_CONV_W:ROW_CONV_W + 4], INV, None, ALU.mult)
                state = prm[:, :, ROW_CONV_STATE:ROW_CONV_STATE + 24].rearrange("p c (s k) -> p c s k", k=3)
                for k in range(3):
                    w = prm[:, :, ROW_CONV_W + k:ROW_CONV_W + k + 1].to_broadcast([P, DC, NS])
                    small(g.tensor_tensor(rpre[:] if k == 0 else rtmp[:], state[:, :, :, k], w, ALU.mult))
                    if k:
                        small(g.tensor_tensor(rpre[:], rpre[:], rtmp[:], ALU.add))

            conv_params()
            units = [u for u in range(4 * R_V) if u != 3]
            for n, u in enumerate(units):
                h = (u - 4) % 8
                pool.wait_ge(acc_read, u + 1)
                if u < 2:
                    dst, part = qiT[:, u, :], P
                elif u == 2:
                    dst, part = kiT[0:ID, :], ID
                else:
                    dst, part = (qT if u < 4 * R_K else kT)[:, h, :], P
                g.tensor_tensor(dst, dst, rot[0:part, u % 2, :], ALU.add).then_inc(roped, 1)
                if u == 6:
                    for t in range(2):
                        pool.wait_ge(idx_sum, t + 1)
                        part = score[:, 2 * P * t:2 * P * t + P]
                        g.affine_select(out=part, in_=part, compare_op=ALU.is_ge, fill=OUT_OF_REACH, base=0,
                                        pattern=[[-1, P]], channel_multiplier=1).then_inc(idx_masked, 1)
                if u == 13:
                    for t in range(2):
                        pool.wait_ge(bias_done, t + 1)
                        part = abias[:, 2 * P * t:2 * P * t + P]
                        g.affine_select(out=part, in_=part, compare_op=ALU.is_ge, fill=OUT_OF_REACH, base=0,
                                        pattern=[[-1, P]], channel_multiplier=1).then_inc(bias_masked, 1)
                if u == 18:
                    pool.wait_ge(gix_done, 2)
                    for rows_, dst_, landed in ((a["cache_k"], kgat, kg_in), (a["cache_v"], vgat, vg_in)):
                        src = rows_.rearrange("a n p h d -> (a n p) (h d)")
                        for j in range(4):
                            g.indirect_dma_start(out=dst_[:, j, :], out_offset=None, in_=src,
                                                 in_offset=bass.IndirectOffsetOnAxis(ap=gix[:, j:j + 1], axis=0)
                                                 ).then_inc(landed[j], 16)
            for h in range(H):
                pool.wait_ge(p_rcp, h + 1)
                for t in range(2):
                    part = slice(0, P) if t == 0 else slice(P, 384)
                    g.tensor_scalar(lg[:, h % 2, part], lg[:, h % 2, part], prcp[:, h % 2, t:t + 1], None, ALU.mult).then_inc(p_norm, 1)

            def ffn_params(layer):
                pool.wait_ge(fprm_kept, layer + 1)
                f = fprm[layer]
                g.tensor_scalar(fw[layer][:], f[:, :, FROW_W:FROW_W + 3], INV, None, ALU.mult)
                state = f[:, :, 0:16].rearrange("p c (s k) -> p c s k", k=2)
                small(g.tensor_tensor(fpre[layer][:], state[:, :, :, 0], f[:, :, FROW_W:FROW_W + 1].to_broadcast([P, FC, NS]), ALU.mult))
                small(g.tensor_tensor(ftmp[:], state[:, :, :, 1], f[:, :, FROW_W + 1:FROW_W + 2].to_broadcast([P, FC, NS]), ALU.mult))
                small(g.tensor_tensor(fpre[layer][:], fpre[layer][:], ftmp[:], ALU.add))
                g.tensor_copy(ftmp[:, 0:1, :], fpre[layer][:, 0:1, :]).then_inc(prm_ready, 1)

            pool.wait_ge(so_done, 1)
            pool.wait_ge(o_mm, H)
            for i, w in enumerate(("w_gate_a", "w_gate_x")):
                pool.dma_start(gstage[:, i, :, :], a[w][0].rearrange("n c d -> c n d")).then_inc(g_in, 16)
            ffn_params(0)
            ffn_params(1)
            add_squares(1)

            def down_squares(layer):
                k = 2 + 2 * layer
                add_square(DC * k, 0, k)
                add_square(DC * k + 1, 1, False)
                with pool.Fori(1, 4) as i:
                    for p in range(2):
                        add_square(i * 2 + (DC * k + p), p, False)

            down_squares(0)
            for n in range(DC):
                pool.wait_ge(gate_sig, n + 1)
                g.tensor_tensor(ix[:, n, :], gates[:, n % 2, 1, :], xc[:, n, :], ALU.mult).then_inc(ix_done, 1)
            add_squares(3)
            down_squares(1)


_INS = ["x_prompt", "x_sample", "cache_k", "cache_v", "cache_kidx", "state_lru_h", "state_lru_conv", "state_ffn_conv",
        "page_table", "norm_mix", "norm_ffn", "norm_final", "w_attn_in", "w_attn_out", "w_rec_in", "w_rec_conv",
        "b_rec_conv", "w_gate_a", "b_gate_a", "w_gate_x", "b_gate_x", "lru_lambda", "w_rec_out", "w_ffn_up",
        "w_ffn_conv", "b_ffn_conv", "w_ffn_down"]
_OUTS = [("y_prompt", (1, TP, D)), ("y_sample", (NS, 1, D)), ("new_k_prompt", (1, 1, TP, H, P)),
         ("new_v_prompt", (1, 1, TP, H, P)), ("new_kidx_prompt", (1, 1, TP, ID)), ("new_k_sample", (1, NS, 1, H, P)),
         ("new_v_sample", (1, NS, 1, H, P)), ("new_kidx_sample", (1, NS, 1, ID)), ("lru_h_prompt", (1, 1, D)),
         ("lru_conv_prompt", (1, 1, 3, D)), ("lru_h_sample", (1, NS, D)), ("lru_conv_sample", (1, NS, 3, D)),
         ("ffn_conv_prompt", (2, 1, 2, DFF)), ("ffn_conv_sample", (2, NS, 2, DFF))]


def constants():
    import numpy as np
    f = np.float32
    ca = np.zeros((P, CA_W), f)
    ca[:, CA_IDENT:CA_IDENT + P] = np.eye(P, dtype=f)
    pos = np.concatenate([np.arange(TP), np.full(NS, PAST)]).astype(f)
    for width, c0, s0 in ((P, CA_COSH, CA_SINH), (ID, CA_COSI, CA_SINI)):
        half = width // 2
        inv = f(10000.0) ** (-np.arange(half, dtype=f) * f(2.0) / f(width))
        ang = pos[:, None] * inv[None, :].astype(f)
        cos, sin = np.cos(ang).astype(f).T / f(WSCALE), np.sin(ang).astype(f).T / f(WSCALE)
        for b in range(0, P, half):
            ca[b:b + half, c0:c0 + T] = cos
            ca[b:b + half, s0:s0 + T] = sin if b // half % 2 == 0 else -sin
    ca[:, CA_IOTA] = np.arange(P)
    cb = np.zeros((32, CB_W), f)
    for j in range(4):
        for half in range(2):
            cb[2 * j + half, CB_PAIR + j * P + 64 * half:CB_PAIR + j * P + 64 * half + 64] = 1
    for r in range(32):
        cb[r % IH, CB_REP + r] = 1
        cb[r, CB_SAME + r // IH] = 1
    for h in range(H):
        cb[h, CB_HEAD + 8 * h:CB_HEAD + 8 * h + 8] = 1
    return {"const_a": ca, "const_b": cb}


def kernel(**inputs):
    import numpy as _np
    import concourse.bacc as _bacc
    from concourse import mybir as _mybir
    from concourse.bass_utils import run_bass_kernel_spmd as _run

    nc = _bacc.Bacc("TRN2", target_bir_lowering=False, num_devices=1)
    arrays, ins, outs = {}, {}, {}
    for name, x in [(n, inputs[n]) for n in _INS] + list(constants().items()):
        x = _np.ascontiguousarray(x)
        arrays[f"in_{name}"] = x
        ins[name] = nc.dram_tensor(f"in_{name}", x.shape, _mybir.dt.from_np(x.dtype), kind="ExternalInput").ap()
    for name, shape in _OUTS:
        outs[name] = nc.dram_tensor(f"out_{name}", shape, F32, kind="ExternalOutput").ap()
    build(nc, ins, outs)
    r = _run(nc, [arrays], core_ids=[0])
    return tuple(r.results[0][f"out_{name}"] for name, _ in _OUTS)
```
